# Optimizing a Trainium2 kernel written in Bass

```python
import math
import jax, jax.numpy as jnp
from jax import lax
import numpy as np

D_MODEL = 2048
BATCH = 1
SEQ = 256
DEPTH = 2

N_DIFF_HEADS = 4
DIFF_HEAD_DIM = 128
DIFF_V_DIM = 2 * DIFF_HEAD_DIM
N_DIFF_MAPS = 2 * N_DIFF_HEADS
Q_BLOCK = 128
N_RET_HEADS = 4
RET_KEY_DIM = 256
RET_V_DIM = 256
RET_CHUNK = 128
ROPE_BASE = 10000.0
NUM_BUCKETS = 32
MAX_DISTANCE = 128
POOL_WINDOWS = (2, 4, 8, 16)
N_POOL_GROUPS = 4
POOL_GROUP_DIM = D_MODEL // N_POOL_GROUPS
D_FF = 5632
CONV_WIDTH = 3
EPS = 1e-6
NEG_INF = -1e30
DIFF_QK_WIDTH = N_DIFF_HEADS * 2 * DIFF_HEAD_DIM
DIFF_V_WIDTH = N_DIFF_HEADS * DIFF_V_DIM
RET_QK_WIDTH = N_RET_HEADS * RET_KEY_DIM
RET_V_WIDTH = N_RET_HEADS * RET_V_DIM
IN_SPLITS = (DIFF_QK_WIDTH, DIFF_QK_WIDTH, DIFF_V_WIDTH,
             RET_QK_WIDTH, RET_QK_WIDTH, RET_V_WIDTH, RET_V_WIDTH)
IN_WIDTH = sum(IN_SPLITS)
MIX_WIDTH = DIFF_V_WIDTH + RET_V_WIDTH
N_PAR_LAYERS = (DEPTH + 1) // 2
N_POOL_LAYERS = DEPTH // 2

kernel_name = "hybrid_diffattn_retention_pool_convffn"

def rms_norm(x, g):
    xf = x.astype(jnp.float32)
    y = xf * lax.rsqrt(jnp.mean(xf * xf, axis=-1, keepdims=True) + EPS)
    return (y * g.astype(jnp.float32)).astype(x.dtype)

def t5_bucket(dist):
    max_exact = NUM_BUCKETS // 2
    is_small = dist < max_exact
    df = jnp.maximum(dist, 1).astype(jnp.float32)
    large = max_exact + (jnp.log(df / max_exact) / math.log(MAX_DISTANCE / max_exact)
                         * (NUM_BUCKETS - max_exact)).astype(jnp.int32)
    large = jnp.minimum(large, NUM_BUCKETS - 1)
    return jnp.where(is_small, dist, large)

def diff_attention(q, k, v, rel_bias, lam, subln, lam_init):
    B, S, _ = q.shape
    H, M, dh = N_DIFF_HEADS, N_DIFF_MAPS, DIFF_HEAD_DIM
    q = q.reshape(B, S, M, dh).transpose(0, 2, 1, 3).astype(jnp.float32) * (dh ** -0.5)
    k = k.reshape(B, S, M, dh).transpose(0, 2, 1, 3).astype(jnp.float32)
    v = v.reshape(B, S, H, DIFF_V_DIM).transpose(0, 2, 1, 3).astype(jnp.float32)
    n_blk = S // Q_BLOCK
    q_blocks = jnp.moveaxis(q.reshape(B, M, n_blk, Q_BLOCK, dh), 2, 0)
    k_pos = jnp.arange(S)

    def block(args):
        blk, qb = args
        q_pos = blk * Q_BLOCK + jnp.arange(Q_BLOCK)
        dist = q_pos[:, None] - k_pos[None, :]
        bias = rel_bias[t5_bucket(jnp.maximum(dist, 0))]
        s = jnp.einsum('bmqd,bmkd->bmqk', qb, k) + jnp.moveaxis(bias, -1, 0).astype(jnp.float32)
        s = jnp.where(dist[None, None] >= 0, s, NEG_INF)
        p = jax.nn.softmax(s, axis=-1).reshape(B, H, 2, Q_BLOCK, S)
        a = p[:, :, 0] - lam * p[:, :, 1]
        return jnp.einsum('bhqk,bhkd->bhqd', a, v)

    o = lax.map(block, (jnp.arange(n_blk), q_blocks))
    o = jnp.moveaxis(o, 0, 2).reshape(B, H, S, DIFF_V_DIM).transpose(0, 2, 1, 3)
    o = rms_norm(o, subln) * (1.0 - lam_init)
    return o.reshape(B, S, DIFF_V_WIDTH)

def rotary(t, cos, sin):
    half = t.shape[-1] // 2
    t1, t2 = t[..., :half], t[..., half:]
    return jnp.concatenate([t1 * cos - t2 * sin, t1 * sin + t2 * cos], axis=-1)

def retention(q, k, v, g):
    B, S, _ = q.shape
    H, DK, DV, C = N_RET_HEADS, RET_KEY_DIM, RET_V_DIM, RET_CHUNK
    q = q.reshape(B, S, H, DK).transpose(0, 2, 1, 3).astype(jnp.float32)
    k = k.reshape(B, S, H, DK).transpose(0, 2, 1, 3).astype(jnp.float32)
    v = v.reshape(B, S, H, DV).transpose(0, 2, 1, 3).astype(jnp.float32)
    pos = jnp.arange(S, dtype=jnp.float32)
    inv_freq = 1.0 / (ROPE_BASE ** jnp.linspace(0.0, 1.0, DK // 2, dtype=jnp.float32))
    ang = pos[:, None] * inv_freq[None, :]
    cos, sin = jnp.cos(ang), jnp.sin(ang)
    q = rotary(q, cos, sin)
    k = rotary(k, cos, sin) * (DK ** -0.5)
    log_g = jnp.log(1.0 - 2.0 ** (-5.0 - jnp.arange(H, dtype=jnp.float32)))
    idx = jnp.arange(C, dtype=jnp.float32)
    rel = idx[:, None] - idx[None, :]
    inner_decay = jnp.where(rel[None] >= 0,
                            jnp.exp(jnp.maximum(rel, 0.0)[None] * log_g[:, None, None]), 0.0)
    q_decay = jnp.exp((idx + 1.0)[None, :] * log_g[:, None])[..., None]
    k_decay = jnp.exp((C - 1.0 - idx)[None, :] * log_g[:, None])[..., None]
    chunk_decay = jnp.exp(C * log_g)[:, None, None]
    n_chunk = S // C

    def to_chunks(t):
        return jnp.moveaxis(t.reshape(B, H, n_chunk, C, t.shape[-1]), 2, 0)

    def step(state, qkv):
        qc, kc, vc = qkv
        scores = jnp.einsum('bhid,bhjd->bhij', qc, kc) * inner_decay
        out = (jnp.einsum('bhij,bhje->bhie', scores, vc)
               + jnp.einsum('bhid,bhde->bhie', qc * q_decay, state))
        state = state * chunk_decay + jnp.einsum('bhjd,bhje->bhde', kc * k_decay, vc)
        return state, out

    state0 = jnp.zeros((B, H, DK, DV), jnp.float32)
    _, o = lax.scan(step, state0, (to_chunks(q), to_chunks(k), to_chunks(v)))
    o = jnp.moveaxis(o, 0, 2).reshape(B, H, S, DV)
    o = o * lax.rsqrt(jnp.mean(o * o, axis=-1, keepdims=True) + EPS)
    o = o.transpose(0, 2, 1, 3).reshape(B, S, RET_V_WIDTH)
    return o * jax.nn.silu(g.astype(jnp.float32))

def parallel_mixer(h, w_in, w_out, rel_bias, lq1, lk1, lq2, lk2, subln, layer_idx):
    proj = jnp.einsum('bsd,de->bse', h, w_in)
    offs = np.cumsum(IN_SPLITS)[:-1].tolist()
    aq, ak, av, rq, rk, rv, rg = jnp.split(proj, offs, axis=-1)
    lam_init = 0.8 - 0.6 * math.exp(-0.3 * layer_idx)
    lam = (jnp.exp(jnp.sum(lq1.astype(jnp.float32) * lk1.astype(jnp.float32)))
           - jnp.exp(jnp.sum(lq2.astype(jnp.float32) * lk2.astype(jnp.float32))) + lam_init)
    a_out = diff_attention(aq, ak, av, rel_bias, lam, subln, lam_init)
    r_out = retention(rq, rk, rv, rg)
    mixed = jnp.concatenate([a_out, r_out], axis=-1).astype(h.dtype)
    return jnp.einsum('bse,ed->bsd', mixed, w_out)

def pool_mixer(h, w_pool, scale):
    B, S, D = h.shape
    hg = h.astype(jnp.float32).reshape(B, S, N_POOL_GROUPS, POOL_GROUP_DIM)
    cs = jnp.cumsum(hg, axis=1)
    t = jnp.arange(1, S + 1, dtype=jnp.float32)
    groups = []
    for gi, w in enumerate(POOL_WINDOWS):
        c = cs[:, :, gi]
        lagged = jnp.pad(c, ((0, 0), (w, 0), (0, 0)))[:, :S]
        count = jnp.minimum(t, float(w))[None, :, None]
        groups.append((c - lagged) / count - hg[:, :, gi])
    pooled = jnp.stack(groups, axis=2).astype(h.dtype)
    y = jnp.einsum('bsgc,gce->bsge', pooled, w_pool).reshape(B, S, D)
    return y * scale

def conv_ffn(h, w_up, conv_w, conv_b, w_down):
    u = jnp.einsum('bsd,df->bsf', h, w_up)
    S = u.shape[1]
    y = conv_b
    for tap in range(CONV_WIDTH):
        shifted = jnp.pad(u, ((0, 0), (tap, 0), (0, 0)))[:, :S]
        y = y + shifted * conv_w[CONV_WIDTH - 1 - tap]
    val, gate = jnp.split(y, 2, axis=-1)
    return jnp.einsum('bsf,fd->bsd', jax.nn.silu(gate) * val, w_down)

def setup_inputs(seed: int = 0) -> dict:
    key = jax.random.key(seed)
    ks = jax.random.split(key, 20)
    f32 = jnp.float32
    nrm = lambda k, shape, s: jax.random.normal(k, shape, f32) * s
    return {
        "x": nrm(ks[0], (BATCH, SEQ, D_MODEL), 1.0),
        "rel_bias": nrm(ks[1], (NUM_BUCKETS, N_DIFF_MAPS), 0.5),
        "mix_norm": 1.0 + nrm(ks[2], (DEPTH, D_MODEL), 0.02),
        "ffn_norm": 1.0 + nrm(ks[3], (DEPTH, D_MODEL), 0.02),
        "final_norm": 1.0 + nrm(ks[4], (D_MODEL,), 0.02),
        "w_in": nrm(ks[5], (N_PAR_LAYERS, D_MODEL, IN_WIDTH), D_MODEL ** -0.5),
        "w_out": nrm(ks[6], (N_PAR_LAYERS, MIX_WIDTH, D_MODEL), MIX_WIDTH ** -0.5),
        "lam_q1": nrm(ks[7], (N_PAR_LAYERS, DIFF_HEAD_DIM), 0.1),
        "lam_k1": nrm(ks[8], (N_PAR_LAYERS, DIFF_HEAD_DIM), 0.1),
        "lam_q2": nrm(ks[9], (N_PAR_LAYERS, DIFF_HEAD_DIM), 0.1),
        "lam_k2": nrm(ks[10], (N_PAR_LAYERS, DIFF_HEAD_DIM), 0.1),
        "diff_subln": 1.0 + nrm(ks[11], (N_PAR_LAYERS, DIFF_V_DIM), 0.02),
        "pool_w": nrm(ks[12], (N_POOL_LAYERS, N_POOL_GROUPS, POOL_GROUP_DIM, POOL_GROUP_DIM), POOL_GROUP_DIM ** -0.5),
        "pool_scale": 1.0 + nrm(ks[13], (N_POOL_LAYERS, D_MODEL), 0.02),
        "w_up": nrm(ks[14], (DEPTH, D_MODEL, 2 * D_FF), D_MODEL ** -0.5),
        "conv_w": nrm(ks[15], (DEPTH, CONV_WIDTH, 2 * D_FF), CONV_WIDTH ** -0.5),
        "conv_b": nrm(ks[16], (DEPTH, 2 * D_FF), 0.01),
        "w_down": nrm(ks[17], (DEPTH, D_FF, D_MODEL), D_FF ** -0.5),
    }

def reference(x, rel_bias, mix_norm, ffn_norm, final_norm, w_in, w_out, lam_q1, lam_k1,
              lam_q2, lam_k2, diff_subln, pool_w, pool_scale, w_up, conv_w, conv_b, w_down):
    for l in range(DEPTH):
        h = rms_norm(x, mix_norm[l])
        if l % 2 == 0:
            i = l // 2
            x = x + parallel_mixer(h, w_in[i], w_out[i], rel_bias, lam_q1[i], lam_k1[i],
                                   lam_q2[i], lam_k2[i], diff_subln[i], l).astype(x.dtype)
        else:
            j = l // 2
            x = x + pool_mixer(h, pool_w[j], pool_scale[j]).astype(x.dtype)
        h = rms_norm(x, ffn_norm[l])
        x = x + conv_ffn(h, w_up[l], conv_w[l], conv_b[l], w_down[l]).astype(x.dtype)
    return rms_norm(x, final_norm)


_drawn_inputs = setup_inputs


def setup_inputs(seed=0):
    import zlib

    import numpy as np

    out = dict(_drawn_inputs(seed))
    spreads = {}
    factors = {'ffn_norm': 3.319,
     'final_norm': 2.865,
     'lam_k1': 3.146,
     'lam_q2': 3.07,
     'diff_subln': 5.341,
     'pool_scale': 4.934,
     'conv_b': 6.905}
    for name, (base, spread) in spreads.items():
        noise = np.random.default_rng([zlib.crc32(name.encode()), seed]).standard_normal(out[name].shape)
        drawn = base * np.exp(spread * noise) if base else spread * noise
        out[name] = __import__('jax').numpy.asarray(drawn.astype(out[name].dtype))
    for name, factor in factors.items():
        out[name] = (out[name] * factor).astype(out[name].dtype)
    return out
```

```python
import math
from contextlib import ExitStack

import concourse.bass as bass
from concourse import mybir

ALU = mybir.AluOpType
ACT = mybir.ActivationFunctionType
AX = mybir.AxisListType
F32 = mybir.dt.float32
F32R = mybir.dt.float32r

P = 128
EPS = 1e-6
LAM_INIT = 0.8 - 0.6 * math.exp(-0.3 * 0)
POOL_WINDOWS = (2, 4, 8, 16)
RAW_SLOTS = 4
KT = 4


def trunk_kernel(nc, xT, rel_bias, norm_g, w_in, w_out, lam, subln, pool_w, pool_scale,
                 w_up, conv, w_down, bucket_onehot, rot_cos, rot_sin, decay, pool_count, ident_in, flip_in, outT):
    D, S = xT.shape
    DT = D // P
    DEPTH = w_up.shape[0]
    FF = w_down.shape[1]
    FT = FF // P
    COLS = KT * P
    PAIRS = FF // COLS
    DN_UNITS = FF // COLS
    DN_GROUPS = D // COLS
    UP_UNITS = D // COLS
    BD = rel_bias.shape[1]
    NB = rel_bias.shape[0]
    SPAN = bucket_onehot.shape[1]
    QK_SCALE = float(P) ** -0.5
    HEAD_V = 256

    GROUPS = [(0, "f"), (1024, "f"), (2048, "t"), (512, "f"), (1536, "f"), (2560, "t"),
              (3072, "f"), (4096, "f"), (5120, "t"), (3584, "f"), (4608, "f"), (5632, "t"),
              (6144, "f"), (6656, "f")]
    NG_IN = len(GROUPS)
    U_IN = 0
    U_OUT = U_IN + NG_IN * 4
    U_UP = [U_OUT + 16, 0]
    U_DN = [U_UP[0] + 8 * PAIRS, 0]
    U_POOL = U_DN[0] + DN_UNITS * DN_GROUPS
    U_UP[1] = U_POOL + 4
    U_DN[1] = U_UP[1] + 8 * PAIRS
    G_OUT = NG_IN
    G_UP = [G_OUT + 4, 0]
    G_DN = [G_UP[0] + 2 * PAIRS, 0]
    G_POOL = G_DN[0] + DN_GROUPS
    G_UP[1] = G_POOL + 4
    G_DN[1] = G_UP[1] + 2 * PAIRS
    DN_USES = [(DN_UNITS - s + RAW_SLOTS - 1) // RAW_SLOTS for s in range(RAW_SLOTS)]
    R_IN = [0] * 4
    R_OUT = [NG_IN] * 4
    R_UP = [[n + 4 for n in R_OUT], None]
    R_DN = [[n + 2 * PAIRS for n in R_UP[0]], None]
    R_POOL = [n + DN_GROUPS * m for n, m in zip(R_DN[0], DN_USES)]
    R_UP[1] = [n + 1 for n in R_POOL]
    R_DN[1] = [n + 2 * PAIRS for n in R_UP[1]]
    H_BASE = [0, DT, None, 2 * DT]
    SQ_STEPS = 6
    ATTN_START = (12, 15, 24, 27)
    RET_START = (38, 41, 49, 52)

    scratch = nc.dram_tensor("bias_strip", (BD, SPAN), F32, kind="Internal").ap()

    ctx = ExitStack()
    with ctx:
        mixer = ExitStack()

        def sb(name, shape, dt=F32, stack=ctx):
            return stack.enter_context(nc.sbuf_tensor(name, shape, dt))

        x = sb("x", [P, DT, S])
        h = sb("h", [P, DT, 2 * S], F32R)
        raw = sb("raw", [P, RAW_SLOTS, KT, COLS])
        hi = sb("hi", [P, KT, COLS], F32R)
        lo = sb("lo", [P, KT, COLS], F32R)
        sqacc = sb("sqacc", [P, 4, S])
        sqt = sb("sqt", [P, 4, S])
        rstd = sb("rstd", [P, S + 2])
        rms = sb("rms", [P, S + 2])
        gains = sb("gains", [P, 5, DT])
        cw = sb("cw", [P, DEPTH, 2 * FT, 4])
        pscale = sb("pscale", [P, DT])
        pcount = sb("pcount", [P, 4, POOL_WINDOWS[-1]])
        ones = sb("ones", [P, P])
        eps = sb("eps", [P, 1])
        ident = sb("ident", [P, P])
        with mixer:
            qb = [sb(f"q{i}", [P, 4, S], stack=mixer) for i in range(2)]
            kb = [sb(f"k{i}", [P, 4, S], stack=mixer) for i in range(2)]
            vb = [sb(f"v{i}", [P, 2, COLS], stack=mixer) for i in range(2)]
            bias = sb("bias", [P, BD, S], stack=mixer)
            heads = sb("heads", [P, 8, S], stack=mixer)
            mixed = sb("mixed", [P, DT, 2 * S], F32R, stack=mixer)
            ssq = sb("ssq", [P, 4, S], stack=mixer)
            cos = sb("cos", [P, S], stack=mixer)
            sin = sb("sin", [P, S], stack=mixer)
            dec = sb("dec", [P, 4, S], stack=mixer)
            sc = sb("sc", [P, 2, 384], stack=mixer)
            am = sb("am", [P, 384], stack=mixer)
            amT = sb("amT", [P, 384], stack=mixer)
            sqo = sb("sqo", [P, 2, S], stack=mixer)
            rot = sb("rot", [P, 3, S], stack=mixer)
            mt = sb("mt", [P, 2, S], stack=mixer)
            flip = mt[:, 0, 0:P]
            onehot = sb("onehot", [NB + 1, SPAN], stack=mixer)
            relb = sb("relb", [NB + 1, BD], stack=mixer)
            strip = sc[0:BD, 0, :]
            lamv = sb("lamv", [P, 4], stack=mixer)
            lamp = sb("lamp", [P, 4], stack=mixer)
            sub = sb("sub", [P, 2], stack=mixer)
            mx = sb("mx", [P, 4], stack=mixer)
            negmx = sb("negmx", [P, 4], stack=mixer)
            den = sb("den", [P, 4], stack=mixer)
            rden = sb("rden", [P, 4], stack=mixer)
        gate = bias
        CONSTS = [(relb[0:NB, :], rel_bias), (onehot[:, :], bucket_onehot), (lamv[:, :], lam),
                  (gains[:, :, :], norm_g), (ident[:, :], ident_in), (sub[:, :], subln),
                  (cos[:, :], rot_cos), (sin[:, :], rot_sin), (dec[:, :, :], decay), (pscale[:, :], pool_scale),
                  (pcount[:, :, :], pool_count), (flip, flip_in), (cw[:, :, :, :], conv)]
        N_CONST = len(CONSTS)
        act = sb("act", [P, FT, 2 * S], F32R)
        u = sb("u", [P, 4, S])
        yv = sb("yv", [P, 4, S])
        yg = sb("yg", [P, 4, S])
        ps = ctx.enter_context(nc.psum_tensor("ps", [P, 8, 512], F32))

        def sem(name):
            return ctx.enter_context(nc.semaphore(name))

        x_in = [sem(f"x_in{i}") for i in range(4)]
        c_in = sem("c_in")
        raw_full = [sem(f"raw_full{i}") for i in range(RAW_SLOTS)]
        hi_done = sem("hi_done")
        lo_done = sem("lo_done")
        w_used = sem("w_used")
        evacuated = sem("evacuated")
        h_hi = sem("h_hi")
        h_lo = sem("h_lo")
        sq_ready = sem("sq_ready")
        sq_added = sem("sq_added")
        norm_sum = sem("norm_sum")
        rms_done = sem("rms_done")
        rstd_ready = sem("rstd_ready")
        setup = sem("setup")
        strip_mm = sem("strip_mm")
        strip_sb = sem("strip_sb")
        strip_out = sem("strip_out")
        bias_in = sem("bias_in")
        flipped = sem("flipped")
        bias_ready = sem("bias_ready")
        lam_prod = sem("lam_prod")
        lam_sum = sem("lam_sum")
        lam_exp = sem("lam_exp")
        lam_done = sem("lam_done")
        score_mm = sem("score_mm")
        biased = sem("biased")
        rowmax = sem("rowmax")
        negmaxed = sem("negmaxed")
        exped = sem("exped")
        inverted = sem("inverted")
        map1 = sem("map1")
        map2 = sem("map2")
        turned = sem("turned")
        turned_sb = sem("turned_sb")
        rotA = sem("rotA")
        rotated = sem("rotated")
        rscore_mm = sem("rscore_mm")
        decayed = sem("decayed")
        head_mm = sem("head_mm")
        head_kept = sem("head_kept")
        ssq_mm = sem("ssq_mm")
        ssq_kept = sem("ssq_kept")
        head_rms = sem("head_rms")
        head_rstd = sem("head_rstd")
        gated_r = sem("gated_r")
        mix_tmp = sem("mix_tmp")
        mix_f32 = sem("mix_f32")
        mix_hi = sem("mix_hi")
        mix_lo = sem("mix_lo")
        x_half = sem("x_half")
        sum_a = sem("sum_a")
        u_ready = sem("u_ready")
        y0 = sem("y0")
        y1 = sem("y1")
        y2 = sem("y2")
        silu_done = sem("silu_done")
        gated = sem("gated")
        act_hi = sem("act_hi")
        act_lo = sem("act_lo")
        pooled_round = sem("pooled_round")
        pooled_split = sem("pooled_split")
        pool_step = sem("pool_step")
        pooled = sem("pooled")
        out_ready = sem("out_ready")
        out_done = sem("out_done")

        rstd_b = rstd[:, 0:S]
        rstd_4 = rstd_b.unsqueeze(1).to_broadcast([P, 4, S])

        def narrow(G):
            return ps[:, 2 * (G % 2):2 * (G % 2) + 2, :]

        def wide_bank(G):
            return 4 - 4 * (G % 2)

        block = ctx.enter_context(nc.Block())

        @block.sync
        def _(sp):
            def unit(view, k0, cols, u, slot, first):
                if first is not None:
                    sp.wait_ge(lo_done, first)
                sp.dma_start(raw[:, slot], view[:, k0:k0 + KT, cols]).then_inc(raw_full[slot], 16)

            def tiles(w):
                return w.rearrange("(k p) f -> p k f", p=P)

            def free_at(u, j):
                return KT * (u + (min(j - 2, 0) if j < RAW_SLOTS else j - 3))

            sp.dma_start(x[:, 0:4], xT.rearrange("(k p) s -> p k s", p=P)[:, 0:4]).then_inc(x_in[0], 16)
            win = tiles(w_in[0])
            for n in range(U_OUT):
                c = GROUPS[n // 4][0]
                unit(win, 4 * (n % 4), slice(c, c + COLS), n, n % 4, KT * (n - 3) if n >= 4 else None)
            wout = tiles(w_out[0])
            for n in range(16):
                g = n // 4
                unit(wout, 4 * (n % 4), slice(g * COLS, (g + 1) * COLS), U_OUT + n, n % 4, KT * (U_OUT + n - 3))
            for l in range(DEPTH):
                if l == 1:
                    for g in range(4):
                        unit(tiles(pool_w[0, g]), 0, slice(0, COLS), U_POOL + g, g, free_at(U_POOL, g))
                wup, wdn = tiles(w_up[l]), tiles(w_down[l])
                with sp.Fori(0, PAIRS) as i:
                    for gt in range(2):
                        for j in range(UP_UNITS):
                            n = U_UP[l] + 4 * gt + j
                            unit(wup, KT * j, bass.ds(i * COLS + gt * FF, COLS), n, j, i * (8 * KT) + KT * (n - 3))
                with sp.Fori(0, DN_GROUPS) as g:
                    for j in range(DN_UNITS):
                        unit(wdn, KT * j, bass.ds(g * COLS, COLS), U_DN[l], j % 4,
                             g * (DN_UNITS * KT) + free_at(U_DN[l], j))
            sp.wait_ge(out_done, 16 * 4)

        @block.tensor
        def _(pe):
            def wide_unit(n, base, bank, first, last, moving, ready=None):
                for kt in range(KT):
                    pe.wait_ge(lo_done, base + KT * n + kt + 1)
                    if ready is not None:
                        ready(kt)
                    mv = moving(kt)
                    for m in range(4):
                        c = slice(m * P, (m + 1) * P)
                        pe.matmul(ps[:, bank + m, :], hi[:, kt, c], mv, start=first and kt == 0, stop=False,
                                  skip_group_check=True)
                        mm = pe.matmul(ps[:, bank + m, S:2 * S], lo[:, kt, c], mv[:, 0:S], start=False,
                                       stop=last and kt == KT - 1, skip_group_check=True)
                    mm.then_inc(w_used, 1)

            def narrow_unit(n, G, first, last, moving, ready=None):
                acc = narrow(G)
                for kt in range(KT):
                    pe.wait_ge(lo_done, KT * n + kt + 1)
                    if ready is not None:
                        ready(kt)
                    mv = moving(kt)
                    for m in range(4):
                        c = slice(m * P, (m + 1) * P)
                        out = acc[:, m // 2, (m % 2) * S:(m % 2 + 1) * S]
                        pe.matmul(out, hi[:, kt, c], mv[:, 0:S], start=first and kt == 0 and m % 2 == 0,
                                  stop=False, skip_group_check=True)
                        pe.matmul(out, hi[:, kt, c], mv[:, S:2 * S], start=False, stop=False, skip_group_check=True)
                        mm = pe.matmul(out, lo[:, kt, c], mv[:, 0:S], start=False, stop=last and kt == KT - 1,
                                       skip_group_check=True)
                    mm.then_inc(w_used, 1)

            def token_unit(n, G, first, last, j, ready=None):
                acc = narrow(G)
                for kt in range(KT):
                    pe.wait_ge(lo_done, KT * n + kt + 1)
                    if ready is not None:
                        ready(kt)
                    for t in range(2):
                        xh = h[:, KT * j + kt, t * P:(t + 1) * P]
                        xl = h[:, KT * j + kt, S + t * P:S + (t + 1) * P]
                        pe.matmul(acc[:, t, :], xh, hi[:, kt, :], start=first and kt == 0, stop=False,
                                  skip_group_check=True)
                        pe.matmul(acc[:, t, :], xh, lo[:, kt, :], start=False, stop=False, skip_group_check=True)
                        mm = pe.matmul(acc[:, t, :], xl, hi[:, kt, :], start=False, stop=last and kt == KT - 1,
                                       skip_group_check=True)
                    mm.then_inc(w_used, 1)

            def sum_squares(n, bank):
                pe.wait_ge(sq_added, SQ_STEPS * (n + 1))
                pe.wait_ge(sq_ready, 4 * (n + 1))
                parts = [sqacc[:, 0, :]] + [sqt[:, m, :] for m in range(4)]
                for i, part in enumerate(parts):
                    mm = pe.matmul(ps[:, bank, 0:S], ones[:, :], part, start=i == 0, stop=i == 4,
                                   skip_group_check=True)
                if n == 0:
                    for t in range(2):
                        for i, part in enumerate(parts):
                            mm = pe.matmul(ps[:, bank, S + t:S + t + 1], part[:, t * P:(t + 1) * P], ones[:, 0:1],
                                           start=False, stop=i == 4, skip_group_check=True)
                mm.then_inc(norm_sum, 1)

            def scores(a):
                pe.wait_ge(evacuated, 3 * (a // 2) + 2)
                if a:
                    pe.wait_ge(biased, 2 * a)
                else:
                    pe.wait_ge(bias_ready, 1)
                q, k = qb[a // 2], kb[a // 2]
                for m in range(2):
                    t = 2 * (a % 2) + m
                    pe.matmul(ps[:, 4 + m, 0:S], q[:, t, P:2 * P], k[:, t, :], start=True, stop=True,
                              skip_group_check=True)
                    mm = pe.matmul(ps[:, 4 + m, S:S + P], q[:, t, 0:P], k[:, t, 0:P], start=False, stop=True,
                                   skip_group_check=True)
                mm.then_inc(score_mm, 1)

            def turn(a):
                pe.wait_ge(map2, 2 * (a + 1))
                if a:
                    pe.wait_ge(ssq_kept, a)
                for c in range(3):
                    mm = pe.transpose(ps[:, 6, c * P:(c + 1) * P], am[:, c * P:(c + 1) * P], ident[:, :])
                mm.then_inc(turned, 1)

            def attend(a):
                pe.wait_ge(turned_sb, a + 1)
                pe.wait_ge(evacuated, 3 * (a // 2) + 3)
                if a:
                    pe.wait_ge(head_kept, 2 * a)
                v = vb[a // 2]
                for t in range(2):
                    c = slice((a % 2) * HEAD_V + t * P, (a % 2) * HEAD_V + (t + 1) * P)
                    o = ps[:, 7, t * S:(t + 1) * S]
                    pe.matmul(o[:, 0:P], v[:, 0, c], amT[:, 2 * P:3 * P], start=t == 0, stop=True,
                              skip_group_check=True)
                    pe.matmul(o[:, P:2 * P], v[:, 0, c], amT[:, 0:P], start=False, stop=False, skip_group_check=True)
                    mm = pe.matmul(o[:, P:2 * P], v[:, 1, c], amT[:, P:2 * P], start=False, stop=True,
                                   skip_group_check=True)
                mm.then_inc(head_mm, 1)

            def head_squares(n):
                pe.wait_ge(head_kept, 2 * (n + 1))
                if n < 4:
                    pe.wait_ge(turned_sb, n + 1)
                else:
                    pe.wait_ge(ssq_kept, n)
                for t in range(2):
                    mm = pe.matmul(ps[:, 6, 0:S], ones[:, :], sqo[:, t, :], start=t == 0, stop=t == 1,
                                   skip_group_check=True)
                mm.then_inc(ssq_mm, 1)

            def ret_scores(r):
                pe.wait_ge(rotated, 4 * (r // 2) + 2 + (r % 2) + 1)
                if r:
                    pe.wait_ge(decayed, 2 * r)
                else:
                    pe.wait_ge(biased, 8)
                q, k = qb[r // 2], kb[r // 2]
                for t in range(2):
                    i = 2 * (r % 2) + t
                    pe.matmul(ps[:, 4, 0:S], k[:, i, 0:P], q[:, i, :], start=t == 0, stop=t == 1,
                              skip_group_check=True)
                    mm = pe.matmul(ps[:, 4, S:S + P], k[:, i, P:2 * P], q[:, i, P:2 * P], start=False, stop=t == 1,
                                   skip_group_check=True)
                mm.then_inc(rscore_mm, 1)

            def retain(r):
                pe.wait_ge(decayed, 2 * (r + 1))
                pe.wait_ge(evacuated, 6 + 3 * (r // 2) + 3)
                pe.wait_ge(head_kept, 2 * (4 + r))
                v = vb[r // 2]
                for t in range(2):
                    c = slice((r % 2) * HEAD_V + t * P, (r % 2) * HEAD_V + (t + 1) * P)
                    o = ps[:, 7, t * S:(t + 1) * S]
                    pe.matmul(o, v[:, 0, c], sc[:, 0, 0:S], start=t == 0, stop=False, skip_group_check=True)
                    mm = pe.matmul(o[:, P:2 * P], v[:, 1, c], sc[:, 0, S:S + P], start=False, stop=True,
                                   skip_group_check=True)
                mm.then_inc(head_mm, 1)

            pe.wait_ge(c_in, 16 * N_CONST)
            pe.wait_ge(setup, 3)
            pe.matmul(ps[0:BD, 4, 0:SPAN], relb[:, :], onehot[:, :], start=True, stop=True).then_inc(strip_mm, 1)
            pe.wait_ge(lam_prod, 1)
            pe.matmul(ps[:, 5, 0:2], ones[:, :], lamp[:, 0:2], start=True, stop=True).then_inc(lam_sum, 1)

            def h_tile(j):
                def wait(kt):
                    pe.wait_ge(h_lo, KT * j + kt + 1)
                return wait

            for n in range(U_OUT):
                G, j = divmod(n, 4)
                if j == 0 and G >= 2:
                    pe.wait_ge(evacuated, G - 1)
                ready = h_tile(j) if G == 0 else None
                if GROUPS[G][1] == "t":
                    token_unit(n, G, j == 0, j == 3, j, ready)
                else:
                    narrow_unit(n, G, j == 0, j == 3, lambda kt: h[:, KT * j + kt, :], ready)
                if n == 1:
                    sum_squares(0, 7)
                if n == 4:
                    pe.wait_ge(bias_in, 16)
                    pe.wait_ge(strip_sb, 1)
                    pe.wait_ge(lam_exp, 1)
                    pe.wait_ge(rms_done, 1)
                    for c in range(4):
                        mm = pe.matmul(ps[:, 4 + c, :], flip, heads[:, 2 * c:2 * c + 2, :], start=True, stop=True)
                    mm.then_inc(flipped, 1)
                for a, at in enumerate(ATTN_START):
                    if n == at:
                        scores(a)
                    if n == at + 2:
                        turn(a)
                    if n == at + 3:
                        attend(a)
                    if n == at + 4:
                        head_squares(a)
                for r, at in enumerate(RET_START):
                    if n == at:
                        ret_scores(r)
                    if n == at + 1:
                        retain(r)
                    if n == at + 2:
                        head_squares(4 + r)

            for g in range(4):
                G = G_OUT + g
                pe.wait_ge(evacuated, G - 1)
                for j in range(4):
                    def mixed_tile(kt, j=j):
                        pe.wait_ge(mix_lo, (KT * j + kt) // 2 + 1)
                    narrow_unit(U_OUT + 4 * g + j, G, j == 0, j == 3, lambda kt: mixed[:, KT * j + kt, :],
                                mixed_tile if g == 0 else None)

            for l in range(DEPTH):
                if l == 1:
                    sum_squares(2, wide_bank(G_POOL) + 3)
                    for g in range(4):
                        pe.wait_ge(evacuated, G_POOL + g - 1)
                        if g == 0:
                            pe.wait_ge(rms_done, 3)
                        pe.wait_ge(pooled_split, g + 1)
                        wide_unit(U_POOL + g, 0, wide_bank(G_POOL + g), True, True, lambda kt: h[:, KT * g + kt, :])

                def up(i, first):
                    for gt in range(2):
                        G = G_UP[l] + gt
                        pe.wait_ge(evacuated, i * 2 + G - 1)
                        if first and gt == 1:
                            pe.wait_ge(rms_done, 2 * l + 2)
                        for j in range(UP_UNITS):
                            def split(kt):
                                pe.wait_ge(h_lo, H_BASE[2 * l + 1] + KT * j + kt + 1)
                            wide_unit(U_UP[l] + 4 * gt + j, i * (8 * KT), wide_bank(G), j == 0, j == UP_UNITS - 1,
                                      lambda kt: h[:, KT * j + kt, :], split if first and gt == 0 else None)
                        if first and gt == 0:
                            pe.wait_ge(evacuated, G)
                            sum_squares(2 * l + 1, wide_bank(G + 1) + 3)

                up(0, True)
                with pe.Fori(1, PAIRS) as i:
                    up(i, False)
                with pe.Fori(0, DN_GROUPS // 2) as i:
                    for half in range(2):
                        G = G_DN[l] + half
                        pe.wait_ge(evacuated, i * 2 + G - 1)
                        for j in range(DN_UNITS):
                            pe.wait_ge(act_lo, l * PAIRS + j + 1)
                            wide_unit(U_DN[l] + DN_UNITS * half + j, i * (2 * DN_UNITS * KT), wide_bank(G), j == 0,
                                      j == DN_UNITS - 1, lambda kt: act[:, KT * j + kt, :])
            sum_squares(4, wide_bank(G_DN[1] + 4) + 3)

        @block.scalar
        def _(sc_e):
            a_ = nc.scalar

            def w_hi(n, base, slot, uses):
                sc_e.wait_ge(raw_full[slot], uses)
                for kt in range(KT):
                    if n:
                        sc_e.wait_ge(w_used, base + KT * (n - 1) + kt + 1)
                    a_.activation(hi[:, kt, :], raw[:, slot, kt, :], ACT.Copy).then_inc(hi_done, 1)

            def h_hi_group(n, g, gain):
                for m in range(4):
                    t = 4 * g + m
                    a_.activation(h[:, t, 0:S], x[:, t, :], ACT.Copy, scale=gains[:, gain, t:t + 1]).then_inc(h_hi, 1)
                square(n, g)

            def square(n, g):
                if g:
                    sc_e.wait_ge(sq_added, SQ_STEPS * n + g + 1)
                elif n:
                    sc_e.wait_ge(norm_sum, n)
                a_.activation(sqt[:, :, :], x[:, 4 * g:4 * g + 4, :], ACT.Square).then_inc(sq_ready, 1)

            def root(n, bank):
                sc_e.wait_ge(norm_sum, n + 1)
                w = S + 2 if n == 0 else S
                a_.activation(rms[:, 0:w], ps[:, bank, 0:w], ACT.Sqrt, scale=1.0 / D, bias=eps[:, :]).then_inc(rms_done, 1)

            def exps(a):
                sc_e.wait_ge(negmaxed, a + 1)
                for b, cols in enumerate((slice(0, S), slice(S, S + P))):
                    for m in range(2):
                        i = 2 * b + m
                        a_.activation(sc[:, m, cols], sc[:, m, cols], ACT.Exp, bias=negmx[:, i:i + 1],
                                      accum_out=den[:, i:i + 1]).then_inc(exped, 1)

            def keep_turned(a):
                sc_e.wait_ge(turned, a + 1)
                if a:
                    sc_e.wait_ge(head_mm, a)
                a_.activation(amT[:, :], ps[:, 6, 0:384], ACT.Copy).then_inc(turned_sb, 1)

            def keep_head(n):
                sc_e.wait_ge(head_mm, n + 1)
                if n == 4:
                    sc_e.wait_ge(mix_f32, 8)
                i = n % 4
                a_.activation(heads[:, 2 * i:2 * i + 2, :], ps[:, 7, :].rearrange("p (t s) -> p t s", t=2),
                              ACT.Copy).then_inc(head_kept, 1)
                if n:
                    sc_e.wait_ge(ssq_mm, n)
                a_.activation(sqo[:, :, :], ps[:, 7, :].rearrange("p (t s) -> p t s", t=2),
                              ACT.Square).then_inc(head_kept, 1)

            def head_root(lo_h, hi_h):
                sc_e.wait_ge(ssq_kept, hi_h)
                c = slice(lo_h % 4, lo_h % 4 + hi_h - lo_h)
                a_.activation(ssq[:, c, :], ssq[:, c, :], ACT.Sqrt, scale=1.0 / HEAD_V, bias=eps[:, :]).then_inc(head_rms, 1)

            def ret_gate(g):
                sc_e.wait_ge(evacuated, 13 + g)
                a_.activation(gate[:, 4 * g:4 * g + 4, :], gate[:, 4 * g:4 * g + 4, :], ACT.Silu).then_inc(gated_r, 1)

            def mixed_hi(n):
                sc_e.wait_ge(mix_f32, 2 * (n + 1))
                a_.activation(mixed[:, 2 * n:2 * n + 2, 0:S], mt[:, :, :], ACT.Copy).then_inc(mix_hi, 1)

            for dst, src in CONSTS:
                sc_e.dma_start(dst, src).then_inc(c_in, 16)
            for g in range(1, 4):
                sc_e.dma_start(x[:, 4 * g:4 * g + 4], xT.rearrange("(k p) s -> p k s", p=P)[:, 4 * g:4 * g + 4]).then_inc(x_in[g], 16)
            sc_e.wait_ge(strip_mm, 1)
            a_.activation(strip, ps[0:BD, 4, 0:SPAN], ACT.Copy).then_inc(strip_sb, 1)
            sc_e.wait_ge(strip_sb, 1)
            sc_e.dma_start(scratch, strip).then_inc(strip_out, 16)
            sc_e.wait_ge(lam_sum, 1)
            a_.activation(lamp[:, 2:4], ps[:, 5, 0:2], ACT.Exp).then_inc(lam_exp, 1)
            sc_e.wait_ge(strip_out, 16)
            sc_e.dma_start(heads[:, :, :], bass.AP(scratch.tensor, 0, [[1, P], [SPAN, BD], [1, S]])).then_inc(bias_in, 16)

            w_hi(0, 0, 0, 16)
            for g in range(4):
                sc_e.wait_ge(x_in[g], 16)
                h_hi_group(0, g, 0)
            for n in range(1, U_OUT):
                w_hi(n, 0, n % 4, 16 * (n // 4 + 1))
                if n == 2:
                    root(0, 7)
                if n == 5:
                    sc_e.wait_ge(flipped, 1)
                    a_.activation(bias[:, :, :], ps[:, 4:8, :].rearrange("p b (m s) -> p (b m) s", m=2),
                                  ACT.Copy).then_inc(bias_ready, 1)
                for a, at in enumerate(ATTN_START):
                    if n == at + 1:
                        exps(a)
                    if n == at + 3:
                        keep_turned(a)
                    if n == at + 4:
                        keep_head(a)
                for r, at in enumerate(RET_START):
                    if n == at + 2:
                        keep_head(4 + r)
                if n == 33:
                    head_root(0, 4)
                if 34 <= n < 38:
                    mixed_hi(n - 34)
                if n == 53:
                    head_root(4, 6)
                    ret_gate(0)
                if 54 <= n < 56:
                    mixed_hi(4 + n - 54)
            for n in range(16):
                w_hi(U_OUT + n, 0, n % 4, 16 * (R_OUT[0] + n // 4 + 1))
                if n == 0:
                    head_root(6, 8)
                    ret_gate(1)
                if n == 1:
                    mixed_hi(6)
                if n == 2:
                    mixed_hi(7)
                if n >= 4 and n % 4 == 0:
                    sc_e.wait_ge(evacuated, G_OUT + n // 4)
                    h_hi_group(1, n // 4 - 1, 1)

            def conv0(q, i, l, gt):
                y = yg if gt else yv
                sc_e.wait_ge(u_ready, q + 1)
                for m in range(4):
                    t = i * 4 + gt * FT + m
                    a_.activation(y[:, m, :], u[:, m, :], ACT.Identity, scale=cw[:, l, bass.ds(t, 1), 2],
                                  bias=cw[:, l, bass.ds(t, 1), 3]).then_inc(y0, 1)

            def first_half(q, unit_end, G):
                sc_e.wait_ge(w_used, unit_end)
                sc_e.wait_ge(y2, q * 4)
                b = wide_bank(G)
                a_.activation(u[:, :, :], ps[:, b:b + 4, 0:S], ACT.Copy).then_inc(sum_a, 1)

            def silu(q):
                sc_e.wait_ge(y2, q * 4 + 4)
                a_.activation(yg[:, :, :], yg[:, :, :], ACT.Silu).then_inc(silu_done, 1)

            def act_hi_pair(p, i):
                sc_e.wait_ge(gated, p + 1)
                a_.activation(act[:, bass.ds(i * 4, 4), 0:S], yv[:, :, :], ACT.Copy).then_inc(act_hi, 1)

            for l in range(DEPTH):
                if l == 1:
                    w_hi(U_POOL, 0, 0, 16 * (R_POOL[0] + 1))
                    sc_e.wait_ge(evacuated, G_DN[0] + 4)
                    square(2, 3)
                    root(2, wide_bank(G_POOL) + 3)

                    def pooled_hi(g):
                        sc_e.wait_ge(pooled, g + 1)
                        a_.activation(h[:, 4 * g:4 * g + 4, 0:S], u[:, :, :], ACT.Copy).then_inc(pooled_round, 1)

                    pooled_hi(0)
                    pooled_hi(1)
                    for g in range(1, 4):
                        w_hi(U_POOL + g, 0, g, 16 * (R_POOL[g] + 1))
                        sc_e.wait_ge(evacuated, G_POOL + g)
                        h_hi_group(3, g - 1, 3)
                        if g < 3:
                            pooled_hi(g + 1)

                def up_windows(i, kind, q0, p0):
                    for j in range(UP_UNITS):
                        n = U_UP[l] + 4 * kind + j
                        w_hi(n, i * (8 * KT), j, (i * 2 + (R_UP[l][j] + kind + 1)) * 16)
                        yield j

                def v_windows(i, peel):
                    q = i * 2 + (l * 2 * PAIRS - 1)
                    for j in up_windows(i, 0, None, None):
                        if peel:
                            if j == 0:
                                sc_e.wait_ge(evacuated, G_UP[l])
                                h_hi_group(2 * l + 1, 3, 2 * l + 1)
                            continue
                        if j == 0:
                            first_half(q, i * (8 * KT) + KT * U_UP[l], G_UP[l] - 1)
                        if j == 1:
                            conv0(q, i - 1, l, 1)
                        if j == 3:
                            silu(q)

                def g_windows(i, peel):
                    q = i * 2 + (l * 2 * PAIRS)
                    for j in up_windows(i, 1, None, None):
                        if j == 0:
                            if not peel:
                                act_hi_pair(i + (l * PAIRS - 1), i - 1)
                            else:
                                root(2 * l + 1, wide_bank(G_UP[l] + 1) + 3)
                            first_half(q, i * (8 * KT) + KT * (U_UP[l] + 4), G_UP[l])
                        if j == 1:
                            conv0(q, i, l, 0)

                v_windows(0, True)
                g_windows(0, True)
                with sc_e.Fori(1, PAIRS) as i:
                    v_windows(i, False)
                    g_windows(i, False)
                q = (l + 1) * 2 * PAIRS - 1
                for j in range(DN_UNITS):
                    w_hi(U_DN[l] + j, 0, j % 4, 16 * (R_DN[l][j % 4] + j // 4 + 1))
                    if j == 0:
                        first_half(q, KT * U_DN[l], G_DN[l] - 1)
                    if j == 1:
                        conv0(q, PAIRS - 1, l, 1)
                    if j == 3:
                        silu(q)
                    if j == 4:
                        act_hi_pair((l + 1) * PAIRS - 1, PAIRS - 1)
                with sc_e.Fori(1, DN_GROUPS) as g:
                    for j in range(DN_UNITS):
                        s = j % 4
                        w_hi(U_DN[l] + j, g * (DN_UNITS * KT), s, (g * DN_USES[s] + (R_DN[l][s] + j // 4 + 1)) * 16)
                        if j == 1:
                            nn = 2 * l + 2
                            sc_e.wait_ge(evacuated, g + G_DN[l])
                            sc_e.wait_ge(sq_added, g + SQ_STEPS * nn)
                            a_.activation(sqt[:, :, :], x[:, bass.ds(g * 4 - 4, 4), :], ACT.Square).then_inc(sq_ready, 1)
            sc_e.wait_ge(evacuated, G_DN[1] + 4)
            square(4, 3)
            root(4, wide_bank(G_DN[1] + 4) + 3)
            for g in range(4):
                sc_e.wait_ge(out_ready, 4 * (g + 1))
                sc_e.dma_start(outT.rearrange("(k p) s -> p k s", p=P)[:, 4 * g:4 * g + 4], x[:, 4 * g:4 * g + 4]).then_inc(out_done, 16)

        @block.vector
        def _(ve):
            def w_lo(n, base, slot):
                for kt in range(KT):
                    ve.wait_ge(hi_done, base + KT * n + kt + 1)
                    ve.tensor_tensor(lo[:, kt, :], raw[:, slot, kt, :], hi[:, kt, :].bitcast(F32),
                                     ALU.subtract).then_inc(lo_done, 1)

            def h_lo_group(n, g, gain):
                for m in range(4):
                    t = 4 * g + m
                    ve.wait_ge(h_hi, H_BASE[n] + t + 1)
                    ve.scalar_tensor_tensor(h[:, t, S:2 * S], x[:, t, :], gains[:, gain, t:t + 1],
                                            h[:, t, 0:S].bitcast(F32), ALU.mult, ALU.subtract).then_inc(h_lo, 1)

            def invert(n):
                ve.wait_ge(rms_done, n + 1)
                w = S + 2 if n == 0 else S
                ve.reciprocal(rstd[:, 0:w], rms[:, 0:w]).then_inc(rstd_ready, 1)

            def take_out(G):
                ve.wait_ge(w_used, 4 * KT * (G + 1))
                if G == 0:
                    ve.wait_ge(rstd_ready, 1)
                acc = narrow(G)
                part = G // 3
                if GROUPS[G][1] == "t":
                    for t in range(2):
                        i = ve.tensor_scalar(vb[part % 2][:, t, :], acc[:, t, :], rstd[:, S + t:S + t + 1], None, ALU.mult)
                    i.then_inc(evacuated, 1)
                    return
                if G >= 12:
                    ve.wait_ge(biased, 8)
                    dst = gate[:, 4 * (G - 12):4 * (G - 12) + 4, :]
                else:
                    dst = (qb, kb)[G % 3][part % 2][:, :, :]
                ve.tensor_tensor(dst, acc.rearrange("p b (t s) -> p (b t) s", t=2), rstd_4, ALU.mult).then_inc(evacuated, 1)

            def softmax_front(a):
                ve.wait_ge(score_mm, a + 1)
                if a == 0:
                    ve.wait_ge(bias_ready, 1)
                else:
                    ve.wait_ge(map2, 2 * a)
                ve.scalar_tensor_tensor(sc[:, :, 0:S], ps[:, 4:6, 0:S], QK_SCALE, bias[:, 2 * a:2 * a + 2, :],
                                        ALU.mult, ALU.add).then_inc(biased, 1)
                ve.scalar_tensor_tensor(sc[:, :, S:S + P], ps[:, 4:6, S:S + P], QK_SCALE, bias[:, 2 * a:2 * a + 2, P:2 * P],
                                        ALU.mult, ALU.add).then_inc(biased, 1)
                ve.wait_ge(biased, 2 * a + 2)
                ve.tensor_reduce(mx[:, 0:2], sc[:, :, 0:S], AX.X, ALU.max).then_inc(rowmax, 1)
                ve.tensor_reduce(mx[:, 2:4], sc[:, :, S:S + P], AX.X, ALU.max).then_inc(rowmax, 1)
                ve.wait_ge(rowmax, 2 * a + 2)
                ve.tensor_scalar(negmx[:, :], mx[:, :], -1.0, None, ALU.mult).then_inc(negmaxed, 1)

            def softmax_back(a):
                ve.wait_ge(exped, 4 * a + 4)
                ve.reciprocal(rden[:, :], den[:, :]).then_inc(inverted, 1)
                ve.wait_ge(inverted, 2 * a + 1)
                if a == 0:
                    ve.wait_ge(lam_done, 2)
                ve.tensor_scalar(rden[:, 1:4:2], rden[:, 1:4:2], lamv[:, 0:1], None, ALU.mult).then_inc(inverted, 1)
                ve.wait_ge(inverted, 2 * a + 2)
                if a:
                    ve.wait_ge(turned, a)
                for b, cols in enumerate((slice(0, S), slice(S, S + P))):
                    ve.tensor_scalar(am[:, cols], sc[:, 0, cols], rden[:, 2 * b:2 * b + 1], None, ALU.mult).then_inc(map1, 1)
                ve.wait_ge(map1, 2 * a + 2)
                for b, cols in enumerate((slice(0, S), slice(S, S + P))):
                    ve.scalar_tensor_tensor(am[:, cols], sc[:, 1, cols], rden[:, 2 * b + 1:2 * b + 2], am[:, cols],
                                            ALU.mult, ALU.add).then_inc(map2, 1)

            def keep_ssq(n):
                ve.wait_ge(ssq_mm, n + 1)
                if n == 4:
                    ve.wait_ge(mix_f32, 8)
                ve.tensor_copy(ssq[:, n % 4, :], ps[:, 6, 0:S]).then_inc(ssq_kept, 1)

            def invert_heads(k, lo_h, hi_h):
                ve.wait_ge(head_rms, k)
                c = slice(lo_h % 4, lo_h % 4 + hi_h - lo_h)
                ve.reciprocal(ssq[:, c, :], ssq[:, c, :]).then_inc(head_rstd, 1)
                ve.wait_ge(head_rstd, k)

            def mix_attn(n):
                if n:
                    ve.wait_ge(mix_lo, n)
                else:
                    ve.wait_ge(setup, 4)
                for t in range(2):
                    ve.scalar_tensor_tensor(mt[:, t, :], heads[:, 2 * n + t, :], sub[:, t:t + 1], ssq[:, n, :],
                                            ALU.mult, ALU.mult).then_inc(mix_f32, 1)

            def mix_ret(n):
                ve.wait_ge(mix_lo, n)
                ve.wait_ge(gated_r, (n - 4) // 2 + 1)
                i = n - 4
                r = ssq[:, i, :].unsqueeze(1).to_broadcast([P, 2, S])
                ve.tensor_tensor(mt[:, :, :], heads[:, 2 * i:2 * i + 2, :], r, ALU.mult).then_inc(mix_tmp, 1)
                ve.wait_ge(mix_tmp, i + 1)
                ve.tensor_tensor(mt[:, 0, :], mt[:, 0, :], gate[:, 2 * i, :], ALU.mult).then_inc(mix_f32, 1)
                ve.tensor_tensor(mt[:, 1, :], mt[:, 1, :], gate[:, 2 * i + 1, :], ALU.mult).then_inc(mix_f32, 1)

            def mixed_lo(n):
                ve.wait_ge(mix_hi, n + 1)
                ve.wait_ge(mix_f32, 2 * (n + 1))
                ve.tensor_tensor(mixed[:, 2 * n:2 * n + 2, S:2 * S], mt[:, :, :], mixed[:, 2 * n:2 * n + 2, 0:S].bitcast(F32),
                                 ALU.subtract).then_inc(mix_lo, 1)

            def decay_scores(r):
                ve.wait_ge(rscore_mm, r + 1)
                ve.wait_ge(head_mm, 4 + r)
                if r == 0:
                    ve.wait_ge(map2, 8)
                ve.tensor_tensor(sc[:, 0, 0:S], ps[:, 4, 0:S], dec[:, r, :], ALU.mult).then_inc(decayed, 1)
                ve.tensor_tensor(sc[:, 0, S:S + P], ps[:, 4, S:S + P], dec[:, r, 0:P], ALU.mult).then_inc(decayed, 1)

            def add_mixed(g):
                ve.wait_ge(w_used, KT * (U_OUT + 4 * (g + 1)))
                xs = x[:, 4 * g:4 * g + 4, :]
                acc = narrow(G_OUT + g).rearrange("p b (t s) -> p (b t) s", t=2)
                ve.tensor_tensor(xs, acc, xs, ALU.add).then_inc(evacuated, 1)

            ve.memset(ones[:, :], 1.0).then_inc(setup, 1)
            ve.memset(eps[:, :], EPS).then_inc(setup, 1)
            ve.memset(relb[NB:NB + 1, :], 1.0).then_inc(setup, 1)
            ve.wait_ge(c_in, 16 * N_CONST)
            ve.tensor_tensor(lamp[:, 0:2], lamv[:, 0:2], lamv[:, 2:4], ALU.mult).then_inc(lam_prod, 1)
            ve.tensor_scalar(sub[:, :], sub[:, :], 1.0 - LAM_INIT, None, ALU.mult).then_inc(setup, 1)
            w_lo(0, 0, 0)
            for g in range(4):
                h_lo_group(0, g, 0)
            ve.wait_ge(lam_exp, 1)
            ve.tensor_tensor(lamv[:, 1:2], lamp[:, 3:4], lamp[:, 2:3], ALU.subtract).then_inc(lam_done, 1)
            ve.wait_ge(lam_done, 1)
            ve.tensor_scalar(lamv[:, 0:1], lamv[:, 1:2], -LAM_INIT, None, ALU.add).then_inc(lam_done, 1)
            for n in range(1, U_OUT):
                w_lo(n, 0, n % 4)
                if n % 4 == 0:
                    take_out(n // 4 - 1)
                if n == 3:
                    invert(0)
                for a, at in enumerate(ATTN_START):
                    if n == at + 1:
                        softmax_front(a)
                    if n == at + 2:
                        softmax_back(a)
                    if n == at + 5:
                        keep_ssq(a)
                for r, at in enumerate(RET_START):
                    if n == at + 1:
                        decay_scores(r)
                    if n == at + 3:
                        keep_ssq(4 + r)
                if n == 33:
                    invert_heads(1, 0, 4)
                if 35 <= n < 39:
                    mixed_lo(n - 35)
                if 34 <= n < 38:
                    mix_attn(n - 34)
                if n == 54:
                    invert_heads(2, 4, 6)
                    mix_ret(4)
                if n == 55:
                    mixed_lo(4)
                    mix_ret(5)
            for n in range(16):
                w_lo(U_OUT + n, 0, n % 4)
                if n == 0:
                    take_out(13)
                    mixed_lo(5)
                if n == 1:
                    invert_heads(3, 6, 8)
                    mix_ret(6)
                if n == 2:
                    mixed_lo(6)
                    mix_ret(7)
                    mixed_lo(7)
                if n >= 4 and n % 4 == 0:
                    add_mixed(n // 4 - 1)
                    h_lo_group(1, n // 4 - 1, 1)

            def up_sum(q, Gv, Gp):
                b = wide_bank(Gp)
                ve.wait_ge(sum_a, q + 1)
                ve.tensor_tensor(u[:, :, :], u[:, :, :], ps[:, b:b + 4, S:2 * S], ALU.add).then_inc(evacuated, 1)
                ve.wait_ge(evacuated, Gv + 1)
                ve.tensor_tensor(u[:, :, :], u[:, :, :], rstd_4, ALU.mult).then_inc(u_ready, 1)

            def tap1(q, i, l, gt):
                y = yg if gt else yv
                for m in range(4):
                    t = i * 4 + gt * FT + m
                    ve.wait_ge(y0, q * 4 + m + 1)
                    ve.scalar_tensor_tensor(y[:, m, 1:S], u[:, m, 0:S - 1], cw[:, l, bass.ds(t, 1), 1], y[:, m, 1:S],
                                            ALU.mult, ALU.add).then_inc(y1, 1)

            def tap0(q, i, l, gt):
                y = yg if gt else yv
                for m in range(4):
                    t = i * 4 + gt * FT + m
                    ve.wait_ge(y1, q * 4 + m + 1)
                    ve.scalar_tensor_tensor(y[:, m, 2:S], u[:, m, 0:S - 2], cw[:, l, bass.ds(t, 1), 0], y[:, m, 2:S],
                                            ALU.mult, ALU.add).then_inc(y2, 1)

            def gate_values(p):
                ve.wait_ge(silu_done, p + 1)
                ve.tensor_tensor(yv[:, :, :], yv[:, :, :], yg[:, :, :], ALU.mult).then_inc(gated, 1)

            def act_lo_pair(p, i):
                ve.wait_ge(act_hi, p + 1)
                ve.wait_ge(gated, p + 1)
                ve.tensor_tensor(act[:, bass.ds(i * 4, 4), S:2 * S], yv[:, :, :],
                                 act[:, bass.ds(i * 4, 4), 0:S].bitcast(F32), ALU.subtract).then_inc(act_lo, 1)

            def add_down(l, g):
                ve.wait_ge(w_used, KT * (U_DN[l] + DN_UNITS * (g + 1)))
                b, xs = wide_bank(G_DN[l] + g), x[:, 4 * g:4 * g + 4, :]
                ve.tensor_tensor(xs, ps[:, b:b + 4, 0:S], xs, ALU.add).then_inc(x_half, 1)
                ve.wait_ge(x_half, 4 * l + g + 1)
                ve.tensor_tensor(xs, ps[:, b:b + 4, S:2 * S], xs, ALU.add).then_inc(evacuated, 1)

            for l in range(DEPTH):
                if l == 1:
                    w_lo(U_POOL, 0, 0)
                    add_down(0, 3)
                    invert(2)
                    steps = [0]

                    def step(ins):
                        ins.then_inc(pool_step, 1)
                        steps[0] += 1
                        ve.wait_ge(pool_step, steps[0])

                    def pool(g):
                        hn, a, b = yg, yv, u
                        if g:
                            ve.wait_ge(pooled_split, g)
                        for m in range(4):
                            t = 4 * g + m
                            i_ = ve.scalar_tensor_tensor(hn[:, m, :], x[:, t, :], gains[:, 2, t:t + 1], rstd_b, ALU.mult, ALU.mult)
                        step(i_)
                        w, cur, nxt = 1, hn, a
                        while w < POOL_WINDOWS[g]:
                            ve.tensor_copy(nxt[:, :, 0:w], cur[:, :, 0:w])
                            step(ve.tensor_tensor(nxt[:, :, w:S], cur[:, :, w:S], cur[:, :, 0:S - w], ALU.add))
                            cur, nxt = nxt, (b if nxt is a else a)
                            w *= 2
                        few = pcount[:, g, 0:w].unsqueeze(1).to_broadcast([P, 4, w])
                        ve.tensor_tensor(a[:, :, 0:w], cur[:, :, 0:w], few, ALU.mult)
                        step(ve.tensor_scalar(a[:, :, w:S], cur[:, :, w:S], 1.0 / w, None, ALU.mult))
                        ve.tensor_tensor(u[:, :, :], a[:, :, :], hn[:, :, :], ALU.subtract).then_inc(pooled, 1)

                    def pooled_lo(g):
                        ve.wait_ge(pooled, g + 1)
                        ve.wait_ge(pooled_round, g + 1)
                        ve.tensor_tensor(h[:, 4 * g:4 * g + 4, S:2 * S], u[:, :, :], h[:, 4 * g:4 * g + 4, 0:S].bitcast(F32),
                                         ALU.subtract).then_inc(pooled_split, 1)

                    def pool_out(g):
                        ve.wait_ge(w_used, KT * (U_POOL + g + 1))
                        b = wide_bank(G_POOL + g)
                        for m in range(4):
                            t = 4 * g + m
                            i_ = ve.scalar_tensor_tensor(x[:, t, :], ps[:, b + m, 0:S], pscale[:, t:t + 1], x[:, t, :],
                                                         ALU.mult, ALU.add)
                        step(i_)
                        for m in range(4):
                            t = 4 * g + m
                            i_ = ve.scalar_tensor_tensor(x[:, t, :], ps[:, b + m, S:2 * S], pscale[:, t:t + 1], x[:, t, :],
                                                         ALU.mult, ALU.add)
                        i_.then_inc(evacuated, 1)

                    ve.wait_ge(rstd_ready, 3)
                    pool(0)
                    pooled_lo(0)
                    pool(1)
                    pooled_lo(1)
                    for g in range(1, 4):
                        w_lo(U_POOL + g, 0, g)
                        pool_out(g - 1)
                        h_lo_group(3, g - 1, 3)
                        if g < 3:
                            pool(g + 1)
                            pooled_lo(g + 1)

                def v_windows(i, peel):
                    q = i * 2 + (l * 2 * PAIRS - 1)
                    for j in range(UP_UNITS):
                        w_lo(U_UP[l] + j, i * (8 * KT), j)
                        if peel:
                            if j == 0:
                                if l == 0:
                                    add_mixed(3)
                                else:
                                    pool_out(3)
                                h_lo_group(2 * l + 1, 3, 2 * l + 1)
                            continue
                        if j == 0:
                            up_sum(q, i * 2 + (G_UP[l] - 1), G_UP[l] - 1)
                        if j == 1:
                            tap1(q, i - 1, l, 1)
                        if j == 2:
                            tap0(q, i - 1, l, 1)
                        if j == 3:
                            gate_values(i + (l * PAIRS - 1))

                def g_windows(i, peel):
                    q = i * 2 + (l * 2 * PAIRS)
                    for j in range(UP_UNITS):
                        w_lo(U_UP[l] + 4 + j, i * (8 * KT), j)
                        if j == 0:
                            if peel:
                                invert(2 * l + 1)
                                ve.wait_ge(rstd_ready, 2 * l + 2)
                            else:
                                act_lo_pair(i + (l * PAIRS - 1), i - 1)
                            up_sum(q, i * 2 + G_UP[l], G_UP[l])
                        if j == 1:
                            tap1(q, i, l, 0)
                        if j == 2:
                            tap0(q, i, l, 0)

                v_windows(0, True)
                g_windows(0, True)
                with ve.Fori(1, PAIRS) as i:
                    v_windows(i, False)
                    g_windows(i, False)
                q = (l + 1) * 2 * PAIRS - 1
                for j in range(DN_UNITS):
                    w_lo(U_DN[l] + j, 0, j % 4)
                    if j == 0:
                        up_sum(q, G_DN[l] - 1, G_DN[l] - 1)
                    if j == 1:
                        tap1(q, PAIRS - 1, l, 1)
                    if j == 2:
                        tap0(q, PAIRS - 1, l, 1)
                    if j == 3:
                        gate_values((l + 1) * PAIRS - 1)
                    if j == 4:
                        act_lo_pair((l + 1) * PAIRS - 1, PAIRS - 1)
                for g in range(1, DN_GROUPS):
                    for j in range(DN_UNITS):
                        w_lo(U_DN[l] + DN_UNITS * g + j, 0, j % 4)
                        if j == 0:
                            add_down(l, g - 1)
            add_down(1, 3)
            invert(4)
            ve.wait_ge(rstd_ready, 5)
            for t in range(DT):
                ve.scalar_tensor_tensor(x[:, t, :], x[:, t, :], gains[:, 4, t:t + 1], rstd_b, ALU.mult, ALU.mult).then_inc(out_ready, 1)

        @block.gpsimd
        def _(pool_e):
            g_ = nc.gpsimd
            rot_n = [0]

            def sum_sq(n):
                if n:
                    pool_e.wait_ge(norm_sum, n)
                g_.memset(sqacc[:, :, :], 0.0).then_inc(sq_added, 1)
                for g in range(3):
                    pool_e.wait_ge(sq_ready, 4 * n + g + 1)
                    pool_e.wait_ge(sq_added, SQ_STEPS * n + g + 1)
                    g_.tensor_tensor(sqacc[:, :, :], sqacc[:, :, :], sqt[:, :, :], ALU.add).then_inc(sq_added, 1)
                pool_e.wait_ge(sq_added, SQ_STEPS * n + 4)
                g_.tensor_tensor(sqacc[:, 0:2, :], sqacc[:, 0:2, :], sqacc[:, 2:4, :], ALU.add).then_inc(sq_added, 1)
                pool_e.wait_ge(sq_added, SQ_STEPS * n + 5)
                g_.tensor_tensor(sqacc[:, 0, :], sqacc[:, 0, :], sqacc[:, 1, :], ALU.add).then_inc(sq_added, 1)

            def rotate(buf, i):
                t1, t2 = buf[:, 2 * i, :], buf[:, 2 * i + 1, :]

                def mark(ins):
                    ins.then_inc(rotA, 1)
                    rot_n[0] += 1
                if rot_n[0]:
                    pool_e.wait_ge(rotated, rot_n[0])
                g_.tensor_tensor(rot[:, 0, :], t1, cos[:, :], ALU.mult)
                g_.tensor_tensor(rot[:, 1, :], t2, sin[:, :], ALU.mult)
                g_.tensor_tensor(rot[:, 2, :], t1, sin[:, :], ALU.mult)
                mark(g_.tensor_tensor(t2, t2, cos[:, :], ALU.mult))
                pool_e.wait_ge(rotA, rot_n[0])
                g_.tensor_tensor(t1, rot[:, 0, :], rot[:, 1, :], ALU.subtract)
                g_.tensor_tensor(t2, rot[:, 2, :], t2, ALU.add).then_inc(rotated, 1)

            sum_sq(0)
            pool_e.wait_ge(c_in, 16 * N_CONST)
            for part in range(2):
                pool_e.wait_ge(evacuated, 6 + 3 * part + 1)
                rotate(qb[part], 0)
                rotate(qb[part], 1)
                pool_e.wait_ge(evacuated, 6 + 3 * part + 2)
                rotate(kb[part], 0)
                rotate(kb[part], 1)
            for n in range(1, 5):
                sum_sq(n)


def _constants(S):
    import numpy as np
    nb, max_dist, span = 32, 128, 384
    dist = 255 - np.arange(span)
    d = np.maximum(dist, 0)
    large = 16 + (np.log(np.maximum(d, 1).astype(np.float32) / np.float32(16)) / np.float32(math.log(max_dist / 16))
                  * np.float32(nb - 16)).astype(np.int32)
    bucket = np.where(d < 16, d, np.minimum(large, nb - 1))
    onehot = np.zeros((nb + 1, span), np.float32)
    onehot[bucket[dist >= 0], np.nonzero(dist >= 0)[0]] = 1.0
    onehot[nb, dist < 0] = -1e30
    inv_freq = (1.0 / (np.float32(10000.0) ** np.linspace(0.0, 1.0, 128, dtype=np.float32))).astype(np.float32)
    ang = inv_freq[:, None] * np.arange(S, dtype=np.float32)[None, :]
    g = 1.0 - 2.0 ** (-5.0 - np.arange(4.0))
    rel = np.arange(S)[None, None, :] - np.arange(128)[:, None, None]
    decay = np.where(rel >= 0, g[None, :, None] ** np.maximum(rel, 0), 0.0) / 16.0
    count = np.stack([1.0 / np.minimum(np.arange(1, 17), w) for w in POOL_WINDOWS])
    return {
        "bucket_onehot": onehot,
        "rot_cos": np.cos(ang.astype(np.float64)).astype(np.float32),
        "rot_sin": np.sin(ang.astype(np.float64)).astype(np.float32),
        "decay": decay.astype(np.float32),
        "pool_count": np.broadcast_to(count.astype(np.float32), (128, 4, 16)).copy(),
        "ident": np.eye(128, dtype=np.float32),
    }


def kernel(**inputs):
    import numpy as np
    import concourse.bacc as _bacc
    from concourse.bass_utils import run_bass_kernel_spmd as _run

    a = {k: np.asarray(v) for k, v in inputs.items()}
    depth = a["w_up"].shape[0]
    S = a["x"].shape[1]

    def by_partition(v):
        return np.moveaxis(v.reshape(*v.shape[:-1], -1, 128), -1, 0)

    consts = _constants(S)
    norms = np.stack([a["mix_norm"][0], a["ffn_norm"][0], a["mix_norm"][1], a["ffn_norm"][1], a["final_norm"]])
    conv = np.concatenate([a["conv_w"], a["conv_b"][:, None, :]], axis=1)
    arrays = {
        "xT": a["x"][0].T,
        "rel_bias": a["rel_bias"],
        "norm_g": by_partition(norms),
        "w_in": a["w_in"],
        "w_out": a["w_out"],
        "lam": np.stack([a["lam_q1"][0], a["lam_q2"][0], a["lam_k1"][0], a["lam_k2"][0]], axis=1),
        "subln": by_partition(a["diff_subln"][0]),
        "pool_w": a["pool_w"],
        "pool_scale": by_partition(a["pool_scale"][0]),
        "w_up": a["w_up"],
        "conv": np.moveaxis(by_partition(conv), 2, -1),
        "w_down": a["w_down"],
        "bucket_onehot": consts["bucket_onehot"],
        "rot_cos": consts["rot_cos"],
        "rot_sin": consts["rot_sin"],
        "decay": consts["decay"],
        "pool_count": consts["pool_count"],
        "ident": consts["ident"],
        "flip": consts["ident"][::-1],
    }
    nc = _bacc.Bacc("TRN2", target_bir_lowering=False, num_devices=1, dynamic_dma_scratch_size=4096)
    feed, args = {}, []
    for name, v in arrays.items():
        v = np.ascontiguousarray(v)
        feed[f"in_{name}"] = v
        args.append(nc.dram_tensor(f"in_{name}", v.shape, mybir.dt.from_np(v.dtype), kind="ExternalInput").ap())
    out = nc.dram_tensor("out_T", (a["x"].shape[2], S), F32, kind="ExternalOutput").ap()
    trunk_kernel(nc, *args, out)
    r = _run(nc, [feed], core_ids=[0])
    return np.ascontiguousarray(r.results[0]["out_T"].T)[None]
```

```python
import math
from contextlib import ExitStack

import concourse.bass as bass
from concourse import mybir

ALU = mybir.AluOpType
ACT = mybir.ActivationFunctionType
AX = mybir.AxisListType
F32 = mybir.dt.float32
F32R = mybir.dt.float32r

P = 128
EPS = 1e-6
LAM_INIT = 0.8 - 0.6 * math.exp(-0.3 * 0)
POOL_WINDOWS = (2, 4, 8, 16)
RAW_SLOTS = 4
KT = 4


def trunk_kernel(nc, xT, rel_bias, norm_g, w_in, w_out, lam, subln, pool_w, pool_scale,
                 w_up, conv, w_down, bucket_onehot, rot_cos, rot_sin, decay, pool_matrix, ident_in, flip_in, outT):
    D, S = xT.shape
    DT = D // P
    DEPTH = w_up.shape[0]
    FF = w_down.shape[1]
    FT = FF // P
    COLS = KT * P
    PAIRS = FF // COLS
    DN_UNITS = FF // COLS
    DN_GROUPS = D // COLS
    UP_UNITS = D // COLS
    BD = rel_bias.shape[1]
    NB = rel_bias.shape[0]
    SPAN = bucket_onehot.shape[1]
    QK_SCALE = float(P) ** -0.5
    HEAD_V = 256

    GROUPS = [(0, "f"), (1024, "f"), (2048, "t"), (512, "f"), (1536, "f"), (2560, "t"),
              (3072, "f"), (4096, "f"), (5120, "t"), (3584, "f"), (4608, "f"), (5632, "t"),
              (6144, "f"), (6656, "f")]
    NG_IN = len(GROUPS)
    U_IN = 0
    U_OUT = U_IN + NG_IN * 4
    U_UP = [U_OUT + 16, 0]
    U_DN = [U_UP[0] + 8 * PAIRS, 0]
    U_POOL = U_DN[0] + DN_UNITS * DN_GROUPS
    U_UP[1] = U_POOL + 4
    U_DN[1] = U_UP[1] + 8 * PAIRS
    G_OUT = NG_IN
    G_UP = [G_OUT + 4, 0]
    G_DN = [G_UP[0] + 2 * PAIRS, 0]
    G_POOL = G_DN[0] + DN_GROUPS
    G_UP[1] = G_POOL + 4
    G_DN[1] = G_UP[1] + 2 * PAIRS
    DN_USES = [(DN_UNITS - s + RAW_SLOTS - 1) // RAW_SLOTS for s in range(RAW_SLOTS)]
    R_IN = [0] * 4
    R_OUT = [NG_IN] * 4
    R_UP = [[n + 4 for n in R_OUT], None]
    R_DN = [[n + 2 * PAIRS for n in R_UP[0]], None]
    R_POOL = [n + DN_GROUPS * m for n, m in zip(R_DN[0], DN_USES)]
    R_UP[1] = [n + 1 for n in R_POOL]
    R_DN[1] = [n + 2 * PAIRS for n in R_UP[1]]
    H_BASE = [0, DT, 2 * DT, 3 * DT]
    NORM_COLS = [slice(0, S + 2), slice(0, S), slice(S, S + 2), slice(0, S), slice(0, S)]
    SQ_GROUPS = [4, 4, 3, 4, 3]
    SQ_BASE = [sum(g + 3 for g in SQ_GROUPS[:n]) for n in range(6)]
    ATTN_START = (12, 15, 24, 27)
    RET_START = (39, 42, 47, 49)

    scratch = nc.dram_tensor("bias_strip", (BD, SPAN), F32, kind="Internal").ap()

    ctx = ExitStack()
    with ctx:
        mixer = ExitStack()

        def sb(name, shape, dt=F32, stack=ctx):
            return stack.enter_context(nc.sbuf_tensor(name, shape, dt))

        x = sb("x", [P, DT, S])
        h = sb("h", [P, DT, 2 * S], F32R)
        raw = sb("raw", [P, RAW_SLOTS, KT, COLS])
        hi = sb("hi", [P, KT, COLS], F32R)
        lo = sb("lo", [P, KT, COLS], F32R)
        sqacc = sb("sqacc", [P, 4, S])
        sqt = sb("sqt", [P, 4, S])
        rstd = sb("rstd", [P, S + 2])
        rms = sb("rms", [P, S + 2])
        gains = sb("gains", [P, 5, DT])
        cw = sb("cw", [P, DEPTH, 2 * FT, 4])
        pscale = sb("pscale", [P, DT])
        pool_m = sb("pool_m", [P, 4, S + P])
        ones = sb("ones", [P, P])
        eps = sb("eps", [P, 1])
        spare = sb("spare", [P, 1])
        ident = sb("ident", [P, P])
        with mixer:
            qb = [sb(f"q{i}", [P, 4, S], stack=mixer) for i in range(2)]
            kb = [sb(f"k{i}", [P, 4, S], stack=mixer) for i in range(2)]
            vb = [sb(f"v{i}", [P, 2, COLS], stack=mixer) for i in range(2)]
            bias = sb("bias", [P, BD, S], stack=mixer)
            heads = sb("heads", [P, 8, S], stack=mixer)
            mixed = sb("mixed", [P, DT, 2 * S], F32R, stack=mixer)
            ssq = sb("ssq", [P, 4, S], stack=mixer)
            cos = sb("cos", [P, S], stack=mixer)
            sin = sb("sin", [P, S], stack=mixer)
            dec = sb("dec", [P, 4, S], stack=mixer)
            sc = sb("sc", [P, 2, 384], stack=mixer)
            am = sb("am", [P, 384], stack=mixer)
            amT = sb("amT", [P, 384], stack=mixer)
            sqo = sb("sqo", [P, 2, S], stack=mixer)
            rot = sb("rot", [P, 3, S], stack=mixer)
            mt = sb("mt", [P, 2, S], stack=mixer)
            flip = mt[:, 0, 0:P]
            onehot = sb("onehot", [NB + 1, SPAN], stack=mixer)
            relb = sb("relb", [NB + 1, BD], stack=mixer)
            strip = sc[0:BD, 0, :]
            lamv = sb("lamv", [P, 4], stack=mixer)
            lamp = sb("lamp", [P, 4], stack=mixer)
            sub = sb("sub", [P, 2], stack=mixer)
            mx = sb("mx", [P, 4], stack=mixer)
            negmx = sb("negmx", [P, 4], stack=mixer)
            den = sb("den", [P, 4], stack=mixer)
            rden = sb("rden", [P, 4], stack=mixer)
        gate = bias
        CONSTS = [(relb[0:NB, :], rel_bias), (onehot[:, :], bucket_onehot), (lamv[:, :], lam),
                  (ident[:, :], ident_in), (sub[:, :], subln), (flip, flip_in)]
        TABLES = [(cos[:, :], rot_cos), (sin[:, :], rot_sin), (dec[:, :, :], decay), (pscale[:, :], pool_scale),
                  (pool_m[:, :, :], pool_matrix), (cw[:, :, :, :], conv)]
        N_CONST = len(CONSTS)
        N_TABLE = len(TABLES)
        act = sb("act", [P, FT, 2 * S], F32R)
        u = sb("u", [P, 4, S])
        yv = sb("yv", [P, 4, S])
        yg = sb("yg", [P, 4, S])
        ps = ctx.enter_context(nc.psum_tensor("ps", [P, 8, 512], F32))

        def sem(name):
            return ctx.enter_context(nc.semaphore(name))

        x_in = [sem(f"x_in{i}") for i in range(4)]
        x_tile = [sem(f"x_tile{i}") for i in range(3)]
        w_tile = [sem(f"w_tile{i}") for i in range(3)]
        g_in = sem("g_in")
        c_in = sem("c_in")
        table_in = sem("table_in")
        raw_full = [sem(f"raw_full{i}") for i in range(RAW_SLOTS)]
        hi_done = sem("hi_done")
        lo_done = sem("lo_done")
        w_used = sem("w_used")
        evacuated = sem("evacuated")
        h_hi = sem("h_hi")
        h_lo = sem("h_lo")
        sq_ready = sem("sq_ready")
        sq_added = sem("sq_added")
        norm_sum = sem("norm_sum")
        rms_done = sem("rms_done")
        rstd_ready = sem("rstd_ready")
        setup = sem("setup")
        strip_mm = sem("strip_mm")
        strip_sb = sem("strip_sb")
        strip_out = sem("strip_out")
        bias_in = sem("bias_in")
        flipped = sem("flipped")
        bias_ready = sem("bias_ready")
        lam_prod = sem("lam_prod")
        lam_sum = sem("lam_sum")
        lam_exp = sem("lam_exp")
        lam_done = sem("lam_done")
        score_mm = sem("score_mm")
        biased = sem("biased")
        rowmax = sem("rowmax")
        negmaxed = sem("negmaxed")
        exped = sem("exped")
        inverted = sem("inverted")
        map1 = sem("map1")
        map2 = sem("map2")
        turned = sem("turned")
        turned_sb = sem("turned_sb")
        rotA = sem("rotA")
        rotated = sem("rotated")
        rscore_mm = sem("rscore_mm")
        decayed = sem("decayed")
        head_mm = sem("head_mm")
        head_kept = sem("head_kept")
        ssq_mm = sem("ssq_mm")
        ssq_kept = sem("ssq_kept")
        head_rms = sem("head_rms")
        head_rstd = sem("head_rstd")
        gated_r = sem("gated_r")
        ret_normed = sem("ret_normed")
        mix_f32 = sem("mix_f32")
        mix_hi = sem("mix_hi")
        mix_lo = sem("mix_lo")
        x_half = sem("x_half")
        sum_a = sem("sum_a")
        u_ready = sem("u_ready")
        y0 = sem("y0")
        y1 = sem("y1")
        y2 = sem("y2")
        silu_done = sem("silu_done")
        gated = sem("gated")
        act_hi = sem("act_hi")
        act_lo = sem("act_lo")
        z_ready = sem("z_ready")
        pooled_mm = sem("pooled_mm")
        last_added = sem("last_added")
        weighted = sem("weighted")
        out_pool = sem("out_pool")
        out_ready = sem("out_ready")
        out_done = sem("out_done")

        rstd_b = rstd[:, 0:S]
        rstd_4 = rstd_b.unsqueeze(1).to_broadcast([P, 4, S])

        def narrow(G):
            return ps[:, 2 * (G % 2):2 * (G % 2) + 2, :]

        def wide_bank(G):
            return 4 - 4 * (G % 2)

        block = ctx.enter_context(nc.Block())

        @block.sync
        def _(sp):
            def unit(view, k0, cols, u, slot, first):
                if first is not None:
                    sp.wait_ge(lo_done, first)
                sp.dma_start(raw[:, slot], view[:, k0:k0 + KT, cols]).then_inc(raw_full[slot], 16)

            def tiles(w):
                return w.rearrange("(k p) f -> p k f", p=P)

            def free_at(u, j):
                return KT * (u + (min(j - 2, 0) if j < RAW_SLOTS else j - 3))

            win = tiles(w_in[0])
            for n in range(U_OUT):
                c = GROUPS[n // 4][0]
                if n == 0:
                    for kt in range(KT):
                        sp.dma_start(x[:, kt], tiles(xT)[:, kt]).then_inc((x_tile + x_in[:1])[kt], 16)
                        sp.dma_start(raw[:, 0, kt], win[:, kt, c:c + COLS]).then_inc((w_tile + raw_full[:1])[kt], 16)
                    continue
                if n < 4:
                    sp.dma_start(x[:, 4 * n:4 * n + 4], tiles(xT)[:, 4 * n:4 * n + 4]).then_inc(x_in[n], 16)
                unit(win, 4 * (n % 4), slice(c, c + COLS), n, n % 4, KT * (n - 3) if n >= 4 else None)
            wout = tiles(w_out[0])
            for n in range(16):
                g = n // 4
                unit(wout, 4 * (n % 4), slice(g * COLS, (g + 1) * COLS), U_OUT + n, n % 4, KT * (U_OUT + n - 3))
            for l in range(DEPTH):
                if l == 1:
                    for g in range(4):
                        unit(tiles(pool_w[0, g]), 0, slice(0, COLS), U_POOL + g, g, free_at(U_POOL, g))
                wup, wdn = tiles(w_up[l]), tiles(w_down[l])
                with sp.Fori(0, PAIRS) as i:
                    for gt in range(2):
                        for j in range(UP_UNITS):
                            n = U_UP[l] + 4 * gt + j
                            unit(wup, KT * j, bass.ds(i * COLS + gt * FF, COLS), n, j, i * (8 * KT) + KT * (n - 3))
                with sp.Fori(0, DN_GROUPS) as g:
                    for j in range(DN_UNITS):
                        unit(wdn, KT * j, bass.ds(g * COLS, COLS), U_DN[l], j % 4,
                             g * (DN_UNITS * KT) + free_at(U_DN[l], j))
            sp.wait_ge(out_done, 16 * 4)

        @block.tensor
        def _(pe):
            def wide_unit(n, base, bank, first, last, moving, ready=None):
                for kt in range(KT):
                    pe.wait_ge(lo_done, base + KT * n + kt + 1)
                    if ready is not None:
                        ready(kt)
                    mv = moving(kt)
                    for m in range(4):
                        c = slice(m * P, (m + 1) * P)
                        pe.matmul(ps[:, bank + m, :], hi[:, kt, c], mv, start=first and kt == 0, stop=False,
                                  skip_group_check=True)
                        mm = pe.matmul(ps[:, bank + m, S:2 * S], lo[:, kt, c], mv[:, 0:S], start=False,
                                       stop=last and kt == KT - 1, skip_group_check=True)
                    mm.then_inc(w_used, 1)

            def narrow_unit(n, G, first, last, moving, ready=None):
                acc = narrow(G)
                for kt in range(KT):
                    pe.wait_ge(lo_done, KT * n + kt + 1)
                    if ready is not None:
                        ready(kt)
                    mv = moving(kt)
                    for m in range(4):
                        c = slice(m * P, (m + 1) * P)
                        out = acc[:, m // 2, (m % 2) * S:(m % 2 + 1) * S]
                        pe.matmul(out, hi[:, kt, c], mv[:, 0:S], start=first and kt == 0 and m % 2 == 0,
                                  stop=False, skip_group_check=True)
                        pe.matmul(out, hi[:, kt, c], mv[:, S:2 * S], start=False, stop=False, skip_group_check=True)
                        mm = pe.matmul(out, lo[:, kt, c], mv[:, 0:S], start=False, stop=last and kt == KT - 1,
                                       skip_group_check=True)
                    mm.then_inc(w_used, 1)

            def token_unit(n, acc, first, last, j, ready=None):
                for kt in range(KT):
                    pe.wait_ge(lo_done, KT * n + kt + 1)
                    if ready is not None:
                        ready(kt)
                    for t in range(2):
                        xh = h[:, KT * j + kt, t * P:(t + 1) * P]
                        xl = h[:, KT * j + kt, S + t * P:S + (t + 1) * P]
                        pe.matmul(acc[:, t, :], xh, hi[:, kt, :], start=first and kt == 0, stop=False,
                                  skip_group_check=True)
                        pe.matmul(acc[:, t, :], xh, lo[:, kt, :], start=False, stop=False, skip_group_check=True)
                        mm = pe.matmul(acc[:, t, :], xl, hi[:, kt, :], start=False, stop=last and kt == KT - 1,
                                       skip_group_check=True)
                    mm.then_inc(w_used, 1)

            def sum_squares(n, bank):
                pe.wait_ge(sq_added, SQ_BASE[n + 1])
                parts = [sqacc[:, 0, :]]
                if SQ_GROUPS[n] == 3:
                    if n < 4:
                        pe.wait_ge(sq_ready, 4 * (n + 1))
                    parts += [sqt[:, m, :] for m in range(4)]
                end = len(parts) - 1
                if n != 2:
                    for i, part in enumerate(parts):
                        if n == 4 and i % 2 == 1:
                            pe.wait_ge(sq_ready, 4 * n + 3 + (i + 1) // 2)
                        mm = pe.matmul(ps[:, bank, 0:S], ones[:, :], part, start=i == 0, stop=i == end,
                                       skip_group_check=True)
                if n in (0, 2):
                    for t in range(2):
                        for i, part in enumerate(parts):
                            mm = pe.matmul(ps[:, bank, S + t:S + t + 1], part[:, t * P:(t + 1) * P], ones[:, 0:1],
                                           start=n == 2 and i == 0 and t == 0, stop=i == end, skip_group_check=True)
                mm.then_inc(norm_sum, 1)

            def scores(a):
                pe.wait_ge(evacuated, 3 * (a // 2) + 2)
                if a:
                    pe.wait_ge(biased, 2 * a)
                else:
                    pe.wait_ge(bias_ready, 1)
                q, k = qb[a // 2], kb[a // 2]
                for m in range(2):
                    t = 2 * (a % 2) + m
                    pe.matmul(ps[:, 4 + m, 0:S], q[:, t, P:2 * P], k[:, t, :], start=True, stop=True,
                              skip_group_check=True)
                    mm = pe.matmul(ps[:, 4 + m, S:S + P], q[:, t, 0:P], k[:, t, 0:P], start=False, stop=True,
                                   skip_group_check=True)
                mm.then_inc(score_mm, 1)

            def turn(a):
                pe.wait_ge(map2, 2 * (a + 1))
                if a:
                    pe.wait_ge(ssq_kept, a)
                for c in range(3):
                    mm = pe.transpose(ps[:, 6, c * P:(c + 1) * P], am[:, c * P:(c + 1) * P], ident[:, :])
                mm.then_inc(turned, 1)

            def attend(a):
                pe.wait_ge(turned_sb, a + 1)
                pe.wait_ge(evacuated, 3 * (a // 2) + 3)
                if a:
                    pe.wait_ge(head_kept, 2 * a)
                v = vb[a // 2]
                for t in range(2):
                    c = slice((a % 2) * HEAD_V + t * P, (a % 2) * HEAD_V + (t + 1) * P)
                    o = ps[:, 7, t * S:(t + 1) * S]
                    pe.matmul(o[:, 0:P], v[:, 0, c], amT[:, 2 * P:3 * P], start=t == 0, stop=True,
                              skip_group_check=True)
                    pe.matmul(o[:, P:2 * P], v[:, 0, c], amT[:, 0:P], start=False, stop=False, skip_group_check=True)
                    mm = pe.matmul(o[:, P:2 * P], v[:, 1, c], amT[:, P:2 * P], start=False, stop=True,
                                   skip_group_check=True)
                mm.then_inc(head_mm, 1)

            def head_squares(n):
                pe.wait_ge(head_kept, 2 * (n + 1))
                if n < 4:
                    pe.wait_ge(turned_sb, n + 1)
                else:
                    pe.wait_ge(ssq_kept, n)
                for t in range(2):
                    mm = pe.matmul(ps[:, 6, 0:S], ones[:, :], sqo[:, t, :], start=t == 0, stop=t == 1,
                                   skip_group_check=True)
                mm.then_inc(ssq_mm, 1)

            def ret_scores(r):
                pe.wait_ge(rotated, 4 * (r // 2) + 2 + (r % 2) + 1)
                if r:
                    pe.wait_ge(decayed, 2 * r)
                else:
                    pe.wait_ge(biased, 8)
                q, k = qb[r // 2], kb[r // 2]
                for t in range(2):
                    i = 2 * (r % 2) + t
                    pe.matmul(ps[:, 4, 0:S], k[:, i, 0:P], q[:, i, :], start=t == 0, stop=t == 1,
                              skip_group_check=True)
                    mm = pe.matmul(ps[:, 4, S:S + P], k[:, i, P:2 * P], q[:, i, P:2 * P], start=False, stop=t == 1,
                                   skip_group_check=True)
                mm.then_inc(rscore_mm, 1)

            def retain(r):
                pe.wait_ge(decayed, 2 * (r + 1))
                pe.wait_ge(evacuated, 6 + 3 * (r // 2) + 3)
                pe.wait_ge(head_kept, 2 * (4 + r))
                v = vb[r // 2]
                for t in range(2):
                    c = slice((r % 2) * HEAD_V + t * P, (r % 2) * HEAD_V + (t + 1) * P)
                    o = ps[:, 7, t * S:(t + 1) * S]
                    pe.matmul(o, v[:, 0, c], sc[:, 0, 0:S], start=t == 0, stop=False, skip_group_check=True)
                    mm = pe.matmul(o[:, P:2 * P], v[:, 1, c], sc[:, 0, S:S + P], start=False, stop=True,
                                   skip_group_check=True)
                mm.then_inc(head_mm, 1)

            def strip_and_lambda():
                pe.wait_ge(c_in, 16 * N_CONST)
                pe.wait_ge(setup, 3)
                pe.matmul(ps[0:BD, 4, 0:SPAN], relb[:, :], onehot[:, :], start=True, stop=True).then_inc(strip_mm, 1)
                pe.wait_ge(lam_prod, 1)
                pe.matmul(ps[:, 5, 0:2], ones[:, :], lamp[:, 0:2], start=True, stop=True).then_inc(lam_sum, 1)

            def h_tile(j):
                def wait(kt):
                    pe.wait_ge(h_lo, KT * j + kt + 1)
                return wait

            for n in range(U_OUT):
                G, j = divmod(n, 4)
                if j == 0 and G >= 2:
                    pe.wait_ge(evacuated, G - 1)
                ready = h_tile(j) if G == 0 else None
                if GROUPS[G][1] == "t":
                    token_unit(n, narrow(G), j == 0, j == 3, j, ready)
                else:
                    narrow_unit(n, G, j == 0, j == 3, lambda kt: h[:, KT * j + kt, :], ready)
                if n == 4:
                    sum_squares(0, 7)
                if n == 5:
                    strip_and_lambda()
                if n == 10:
                    pe.wait_ge(bias_in, 16)
                    pe.wait_ge(strip_sb, 1)
                    pe.wait_ge(lam_exp, 1)
                    pe.wait_ge(rms_done, 1)
                    for c in range(4):
                        mm = pe.matmul(ps[:, 4 + c, :], flip, heads[:, 2 * c:2 * c + 2, :], start=True, stop=True)
                    mm.then_inc(flipped, 1)
                for a, at in enumerate(ATTN_START):
                    if n == at:
                        scores(a)
                    if n == at + 2:
                        turn(a)
                    if n == at + 3:
                        attend(a)
                    if n == at + 4:
                        head_squares(a)
                for r, at in enumerate(RET_START):
                    if n == at:
                        ret_scores(r)
                    if n == at + 1:
                        retain(r)
                    if n == at + 2:
                        head_squares(4 + r)

            for g in range(4):
                G = G_OUT + g
                pe.wait_ge(evacuated, G - 1)
                for j in range(4):
                    def mixed_tile(kt, j=j):
                        pe.wait_ge(mix_lo, (KT * j + kt) // 2 + 1)
                    narrow_unit(U_OUT + 4 * g + j, G, j == 0, j == 3, lambda kt: mixed[:, KT * j + kt, :],
                                mixed_tile if g == 0 else None)

            for l in range(DEPTH):
                if l == 1:
                    def pool_tokens(g):
                        pe.wait_ge(z_ready, 2 * (g + 1))
                        if g == 0:
                            pe.wait_ge(table_in, 16 * N_TABLE)
                        if g == 1:
                            pe.wait_ge(rms_done, 3)
                        if g >= 2:
                            pe.wait_ge(evacuated, G_POOL + g - 1)
                        z, b = (yv, yg)[g % 2], wide_bank(G_POOL + g) + 2
                        z = z.rearrange("p (t k) s -> p t (k s)", t=2)
                        for m in range(4):
                            c = slice(m * P, (m + 1) * P)
                            out = ps[:, b + m // 2, (m % 2) * S:(m % 2 + 1) * S]
                            pe.matmul(out, z[:, 0, c], pool_m[:, g, 0:S], start=m % 2 == 0, stop=False,
                                      skip_group_check=True)
                            mm = pe.matmul(out[:, P:2 * P], z[:, 1, c], pool_m[:, g, S:S + P], start=False, stop=True,
                                           skip_group_check=True)
                        mm.then_inc(pooled_mm, 1)

                    for g in range(4):
                        G = G_POOL + g
                        if g < 2:
                            pe.wait_ge(evacuated, G - 1)
                        else:
                            pe.wait_ge(z_ready, 2 * (g - 1))

                        def pool_h(kt):
                            pe.wait_ge(h_lo, H_BASE[2] + KT * g + kt + 1)
                        token_unit(U_POOL + g, ps[:, wide_bank(G):wide_bank(G) + 2, :], True, True, g, pool_h)
                        if g == 0:
                            sum_squares(2, wide_bank(G_POOL + 1) + 3)
                        else:
                            pool_tokens(g - 1)
                    pool_tokens(3)

                def up(i, first):
                    for gt in range(2):
                        G = G_UP[l] + gt
                        pe.wait_ge(evacuated, i * 2 + G - 1)
                        if first and gt == 1:
                            pe.wait_ge(rms_done, 2 * l + 2)
                        for j in range(UP_UNITS):
                            def split(kt):
                                pe.wait_ge(h_lo, H_BASE[2 * l + 1] + KT * j + kt + 1)
                            wide_unit(U_UP[l] + 4 * gt + j, i * (8 * KT), wide_bank(G), j == 0, j == UP_UNITS - 1,
                                      lambda kt: h[:, KT * j + kt, :], split if first and gt == 0 else None)
                            if first and gt == 0 and j == 2 + l:
                                pe.wait_ge(evacuated, G)
                                sum_squares(2 * l + 1, wide_bank(G + 1) + 3)

                up(0, True)
                with pe.Fori(1, PAIRS) as i:
                    up(i, False)
                with pe.Fori(0, DN_GROUPS // 2) as i:
                    for half in range(2):
                        G = G_DN[l] + half
                        pe.wait_ge(evacuated, i * 2 + G - 1)
                        for j in range(DN_UNITS):
                            pe.wait_ge(act_lo, l * PAIRS + j + 1)
                            wide_unit(U_DN[l] + DN_UNITS * half + j, i * (2 * DN_UNITS * KT), wide_bank(G), j == 0,
                                      j == DN_UNITS - 1, lambda kt: act[:, KT * j + kt, :])
            sum_squares(4, wide_bank(G_DN[1] + 4) + 3)

        @block.scalar
        def _(sc_e):
            a_ = nc.scalar

            def w_hi(n, base, slot, uses):
                sc_e.wait_ge(raw_full[slot], uses)
                for kt in range(KT):
                    if n:
                        sc_e.wait_ge(w_used, base + KT * (n - 1) + kt + 1)
                    a_.activation(hi[:, kt, :], raw[:, slot, kt, :], ACT.Copy).then_inc(hi_done, 1)

            def h_round(n, g, gain):
                for m in range(4):
                    t = g * 4 + m
                    a_.activation(h[:, bass.ds(t, 1), 0:S], x[:, bass.ds(t, 1), :], ACT.Copy,
                                  scale=gains[:, gain, bass.ds(t, 1)]).then_inc(h_hi, 1)

            def h_hi_group(n, g, gain):
                h_round(n, g, gain)
                square(n, g)

            def square(n, g):
                if g:
                    sc_e.wait_ge(sq_added, SQ_BASE[n] + g + 1)
                elif n:
                    sc_e.wait_ge(norm_sum, n)
                a_.activation(sqt[:, :, :], x[:, 4 * g:4 * g + 4, :], ACT.Square).then_inc(sq_ready, 1)

            def root(n, bank):
                sc_e.wait_ge(norm_sum, n + 1)
                w = NORM_COLS[n]
                a_.activation(rms[:, w], ps[:, bank, w], ACT.Sqrt, scale=1.0 / D, bias=eps[:, :]).then_inc(rms_done, 1)

            def exps(a):
                sc_e.wait_ge(negmaxed, a + 1)
                for b, cols in enumerate((slice(0, S), slice(S, S + P))):
                    for m in range(2):
                        i = 2 * b + m
                        a_.activation(sc[:, m, cols], sc[:, m, cols], ACT.Exp, bias=negmx[:, i:i + 1],
                                      accum_out=den[:, i:i + 1]).then_inc(exped, 1)

            def keep_turned(a):
                sc_e.wait_ge(turned, a + 1)
                if a:
                    sc_e.wait_ge(head_mm, a)
                a_.activation(amT[:, :], ps[:, 6, 0:384], ACT.Copy).then_inc(turned_sb, 1)

            def keep_head(n):
                sc_e.wait_ge(head_mm, n + 1)
                if n == 4:
                    sc_e.wait_ge(mix_f32, 8)
                i = n % 4
                a_.activation(heads[:, 2 * i:2 * i + 2, :], ps[:, 7, :].rearrange("p (t s) -> p t s", t=2),
                              ACT.Copy).then_inc(head_kept, 1)
                if n:
                    sc_e.wait_ge(ssq_mm, n)
                a_.activation(sqo[:, :, :], ps[:, 7, :].rearrange("p (t s) -> p t s", t=2),
                              ACT.Square).then_inc(head_kept, 1)

            def head_root(lo_h, hi_h):
                sc_e.wait_ge(ssq_kept, hi_h)
                c = slice(lo_h % 4, lo_h % 4 + hi_h - lo_h)
                a_.activation(ssq[:, c, :], ssq[:, c, :], ACT.Sqrt, scale=1.0 / HEAD_V, bias=eps[:, :]).then_inc(head_rms, 1)

            def ret_gate(g):
                sc_e.wait_ge(evacuated, 13 + g)
                a_.activation(gate[:, 4 * g:4 * g + 4, :], gate[:, 4 * g:4 * g + 4, :], ACT.Silu).then_inc(gated_r, 1)

            def mixed_hi(n):
                sc_e.wait_ge(mix_f32, 2 * (n + 1))
                a_.activation(mixed[:, 2 * n:2 * n + 2, 0:S], mt[:, :, :], ACT.Copy).then_inc(mix_hi, 1)

            sc_e.dma_start(gains[:, :, :], norm_g).then_inc(g_in, 16)
            sc_e.wait_ge(setup, 2)
            a_.activation(spare[:, :], eps[:, :], ACT.Copy)
            sc_e.wait_ge(g_in, 16)
            for kt in range(KT):
                sc_e.wait_ge((x_tile + x_in[:1])[kt], 16)
                a_.activation(h[:, kt, 0:S], x[:, kt, :], ACT.Copy, scale=gains[:, 0, kt:kt + 1]).then_inc(h_hi, 1)
                sc_e.wait_ge((w_tile + raw_full[:1])[kt], 16)
                a_.activation(hi[:, kt, :], raw[:, 0, kt, :], ACT.Copy).then_inc(hi_done, 1)
            square(0, 0)
            for n in range(1, 4):
                sc_e.wait_ge(x_in[n], 16)
                h_round(0, n, 0)
                w_hi(n, 0, n, 16)
                square(0, n)
                if n == 3:
                    for dst, src in CONSTS:
                        sc_e.dma_start(dst, src).then_inc(c_in, 16)
            w_hi(4, 0, 0, 32)
            w_hi(5, 0, 1, 32)
            root(0, 7)
            for n in range(6, U_OUT):
                w_hi(n, 0, n % 4, 16 * (n // 4 + 1))
                if n == 9:
                    for dst, src in TABLES:
                        sc_e.dma_start(dst, src).then_inc(table_in, 16)
                if n == 6:
                    sc_e.wait_ge(strip_mm, 1)
                    a_.activation(strip, ps[0:BD, 4, 0:SPAN], ACT.Copy).then_inc(strip_sb, 1)
                    sc_e.wait_ge(strip_sb, 1)
                    sc_e.dma_start(scratch, strip).then_inc(strip_out, 16)
                    sc_e.wait_ge(lam_sum, 1)
                    a_.activation(lamp[:, 2:4], ps[:, 5, 0:2], ACT.Exp).then_inc(lam_exp, 1)
                if n == 7:
                    sc_e.wait_ge(strip_out, 16)
                    sc_e.dma_start(heads[:, :, :],
                                   bass.AP(scratch.tensor, 0, [[1, P], [SPAN, BD], [1, S]])).then_inc(bias_in, 16)
                if n == 11:
                    sc_e.wait_ge(flipped, 1)
                    a_.activation(bias[:, :, :], ps[:, 4:8, :].rearrange("p b (m s) -> p (b m) s", m=2),
                                  ACT.Copy).then_inc(bias_ready, 1)
                for a, at in enumerate(ATTN_START):
                    if n == at + 1:
                        exps(a)
                    if n == at + 3:
                        keep_turned(a)
                    if n == at + 4:
                        keep_head(a)
                for r, at in enumerate(RET_START):
                    if n == at + 2:
                        keep_head(4 + r)
                if n == 33:
                    head_root(0, 4)
                if n in (34, 36, 38, 40):
                    mixed_hi((n - 34) // 2)
                if n == 46:
                    head_root(4, 6)
                if n == 53:
                    head_root(6, 8)
                if n == 54:
                    ret_gate(0)
            for n in range(16):
                w_hi(U_OUT + n, 0, n % 4, 16 * (R_OUT[0] + n // 4 + 1))
                if n == 0:
                    mixed_hi(4)
                    ret_gate(1)
                if n == 1:
                    mixed_hi(5)
                if n == 2:
                    mixed_hi(6)
                    mixed_hi(7)
                if n >= 4 and n % 4 == 1:
                    sc_e.wait_ge(evacuated, G_OUT + n // 4)
                    h_hi_group(1, n // 4 - 1, 1)

            def conv0(q, i, l, gt):
                y = yg if gt else yv
                sc_e.wait_ge(u_ready, q + 1)
                for m in range(4):
                    t = i * 4 + gt * FT + m
                    a_.activation(y[:, m, :], u[:, m, :], ACT.Identity, scale=cw[:, l, bass.ds(t, 1), 2],
                                  bias=cw[:, l, bass.ds(t, 1), 3]).then_inc(y0, 1)

            def first_half(q, unit_end, G):
                sc_e.wait_ge(w_used, unit_end)
                sc_e.wait_ge(y2, q * 4)
                b = wide_bank(G)
                a_.activation(u[:, :, :], ps[:, b:b + 4, 0:S], ACT.Copy).then_inc(sum_a, 1)

            def silu(q):
                sc_e.wait_ge(y2, q * 4 + 4)
                a_.activation(yg[:, :, :], yg[:, :, :], ACT.Silu).then_inc(silu_done, 1)

            def act_hi_pair(p, i):
                sc_e.wait_ge(gated, p + 1)
                a_.activation(act[:, bass.ds(i * 4, 4), 0:S], yg[:, :, :], ACT.Copy).then_inc(act_hi, 1)

            sc_e.wait_ge(table_in, 16 * N_TABLE)
            for l in range(DEPTH):
                if l == 1:
                    def project_out(g):
                        sc_e.wait_ge(w_used, KT * (U_POOL + g + 1))
                        if g >= 2:
                            sc_e.wait_ge(pooled_mm, g - 1)
                        z, b = (yv, yg)[g % 2], wide_bank(G_POOL + g)
                        z = z.rearrange("p (t k) s -> p t (k s)", t=2)
                        for t in range(2):
                            a_.activation(z[:, t, :], ps[:, b + t, :], ACT.Copy,
                                          scale=rstd[:, S + t:S + t + 1]).then_inc(z_ready, 1)

                    w_hi(U_POOL, 0, 0, 16 * (R_POOL[0] + 1))
                    sc_e.wait_ge(evacuated, G_DN[0] + 4)
                    square(2, 3)
                    h_round(2, 3, 2)
                    w_hi(U_POOL + 1, 0, 1, 16 * (R_POOL[1] + 1))
                    root(2, wide_bank(G_POOL + 1) + 3)
                    sc_e.wait_ge(rstd_ready, 3)
                    project_out(0)
                    w_hi(U_POOL + 2, 0, 2, 16 * (R_POOL[2] + 1))
                    project_out(1)
                    w_hi(U_POOL + 3, 0, 3, 16 * (R_POOL[3] + 1))
                    project_out(2)
                    sc_e.wait_ge(evacuated, G_POOL + 1)
                    h_hi_group(3, 0, 3)

                def up_windows(i, kind):
                    for j in range(UP_UNITS):
                        n = U_UP[l] + 4 * kind + j
                        w_hi(n, i * (8 * KT), j, (i * 2 + (R_UP[l][j] + kind + 1)) * 16)
                        yield j

                def v_windows(i, peel):
                    q = i * 2 + (l * 2 * PAIRS - 1)
                    for j in up_windows(i, 0):
                        if peel:
                            if l == 1 and j == 0:
                                project_out(3)
                                sc_e.wait_ge(evacuated, G_POOL + 2)
                                h_hi_group(3, 1, 3)
                            if l == 1 and j == 1:
                                sc_e.wait_ge(evacuated, G_UP[l] - 1)
                                h_hi_group(3, 2, 3)
                            if j == 3:
                                if l == 0:
                                    root(1, wide_bank(G_UP[0] + 1) + 3)
                                else:
                                    a_.activation(spare[:, :], eps[:, :], ACT.Sqrt)
                            if j == (2 if l else 1):
                                sc_e.wait_ge(evacuated, G_UP[l])
                                h_hi_group(2 * l + 1, 3, 2 * l + 1)
                            continue
                        if j == 0:
                            first_half(q, i * (8 * KT) + KT * U_UP[l], G_UP[l] - 1)
                        if j == 1:
                            conv0(q, i - 1, l, 1)
                        if j == 3:
                            silu(q)

                def g_windows(i, peel):
                    q = i * 2 + (l * 2 * PAIRS)
                    for j in up_windows(i, 1):
                        if j == 2 and not peel:
                            act_hi_pair(i + (l * PAIRS - 1), i - 1)
                        if j == 0:
                            if peel and l == 1:
                                root(3, wide_bank(G_UP[l] + 1) + 3)
                            first_half(q, i * (8 * KT) + KT * (U_UP[l] + 4), G_UP[l])
                        if j == 1:
                            conv0(q, i, l, 0)

                v_windows(0, True)
                g_windows(0, True)
                a_.activation(spare[:, :], eps[:, :], ACT.Silu)
                with sc_e.Fori(1, PAIRS) as i:
                    v_windows(i, False)
                    g_windows(i, False)
                q = (l + 1) * 2 * PAIRS - 1
                for j in range(DN_UNITS):
                    w_hi(U_DN[l] + j, 0, j % 4, 16 * (R_DN[l][j % 4] + j // 4 + 1))
                    if j == 0:
                        first_half(q, KT * U_DN[l], G_DN[l] - 1)
                    if j == 1:
                        conv0(q, PAIRS - 1, l, 1)
                    if j == 3:
                        silu(q)
                    if j == 5:
                        act_hi_pair((l + 1) * PAIRS - 1, PAIRS - 1)
                with sc_e.Fori(1, DN_GROUPS) as g:
                    for j in range(DN_UNITS):
                        s = j % 4
                        w_hi(U_DN[l] + j, g * (DN_UNITS * KT), s, (g * DN_USES[s] + (R_DN[l][s] + j // 4 + 1)) * 16)
                        if j == 2 and l == 0:
                            h_round(2, g - 1, 2)
                        if j == 1:
                            nn = 2 * l + 2
                            sc_e.wait_ge(evacuated, g + G_DN[l])
                            sc_e.wait_ge(sq_added, g + SQ_BASE[nn])
                            a_.activation(sqt[:, :, :], x[:, bass.ds(g * 4 - 4, 4), :], ACT.Square).then_inc(sq_ready, 1)
            sc_e.wait_ge(sq_ready, 4 * 4 + 1)
            for t in range(4):
                last = a_.activation(x[:, t, :], x[:, t, :], ACT.Copy, scale=gains[:, 4, t:t + 1])
            last.then_inc(weighted, 1)
            a_.activation(spare[:, :], eps[:, :], ACT.Sqrt)
            sc_e.wait_ge(sq_added, SQ_BASE[4] + 4)
            for half in range(2):
                m = slice(2 * half, 2 * half + 2)
                sc_e.wait_ge(last_added, half + 1)
                a_.activation(sqt[:, m, :], x[:, 12 + 2 * half:14 + 2 * half, :], ACT.Square).then_inc(sq_ready, 1)
            root(4, wide_bank(G_DN[1] + 4) + 3)
            for g in (1, 2, 0, 3):
                if g == 0:
                    sc_e.wait_ge(out_pool, 1)
                else:
                    sc_e.wait_ge(out_ready, 4 * g)
                sc_e.dma_start(outT.rearrange("(k p) s -> p k s", p=P)[:, 4 * g:4 * g + 4], x[:, 4 * g:4 * g + 4]).then_inc(out_done, 16)

        @block.vector
        def _(ve):
            def w_lo(n, base, slot, kts=range(KT)):
                for kt in kts:
                    ve.wait_ge(hi_done, base + KT * n + kt + 1)
                    ve.tensor_tensor(lo[:, kt, :], raw[:, slot, kt, :], hi[:, kt, :].bitcast(F32),
                                     ALU.subtract).then_inc(lo_done, 1)

            def h_lo_group(n, g, gain, ms=range(4)):
                for m in ms:
                    t = 4 * g + m
                    ve.wait_ge(h_hi, H_BASE[n] + t + 1)
                    ve.scalar_tensor_tensor(h[:, t, S:2 * S], x[:, t, :], gains[:, gain, t:t + 1],
                                            h[:, t, 0:S].bitcast(F32), ALU.mult, ALU.subtract).then_inc(h_lo, 1)

            def invert(n):
                ve.wait_ge(rms_done, n + 1)
                w = NORM_COLS[n]
                ve.reciprocal(rstd[:, w], rms[:, w]).then_inc(rstd_ready, 1)

            def take_out(G):
                ve.wait_ge(w_used, 4 * KT * (G + 1))
                if G == 0:
                    ve.wait_ge(rstd_ready, 1)
                acc = narrow(G)
                part = G // 3
                if GROUPS[G][1] == "t":
                    for t in range(2):
                        i = ve.tensor_scalar(vb[part % 2][:, t, :], acc[:, t, :], rstd[:, S + t:S + t + 1], None, ALU.mult)
                    i.then_inc(evacuated, 1)
                    return
                if G >= 12:
                    ve.wait_ge(biased, 8)
                    dst = gate[:, 4 * (G - 12):4 * (G - 12) + 4, :]
                else:
                    dst = (qb, kb)[G % 3][part % 2][:, :, :]
                ve.tensor_tensor(dst, acc.rearrange("p b (t s) -> p (b t) s", t=2), rstd_4, ALU.mult).then_inc(evacuated, 1)

            def softmax_front(a):
                ve.wait_ge(score_mm, a + 1)
                if a == 0:
                    ve.wait_ge(bias_ready, 1)
                else:
                    ve.wait_ge(map2, 2 * a)
                ve.scalar_tensor_tensor(sc[:, :, 0:S], ps[:, 4:6, 0:S], QK_SCALE, bias[:, 2 * a:2 * a + 2, :],
                                        ALU.mult, ALU.add).then_inc(biased, 1)
                ve.scalar_tensor_tensor(sc[:, :, S:S + P], ps[:, 4:6, S:S + P], QK_SCALE, bias[:, 2 * a:2 * a + 2, P:2 * P],
                                        ALU.mult, ALU.add).then_inc(biased, 1)
                ve.wait_ge(biased, 2 * a + 2)
                ve.tensor_reduce(mx[:, 0:2], sc[:, :, 0:S], AX.X, ALU.max).then_inc(rowmax, 1)
                ve.tensor_reduce(mx[:, 2:4], sc[:, :, S:S + P], AX.X, ALU.max).then_inc(rowmax, 1)
                ve.wait_ge(rowmax, 2 * a + 2)
                ve.tensor_scalar(negmx[:, :], mx[:, :], -1.0, None, ALU.mult).then_inc(negmaxed, 1)

            def softmax_back(a):
                ve.wait_ge(exped, 4 * a + 4)
                ve.reciprocal(rden[:, :], den[:, :]).then_inc(inverted, 1)
                ve.wait_ge(inverted, 2 * a + 1)
                if a == 0:
                    ve.wait_ge(lam_done, 2)
                ve.tensor_scalar(rden[:, 1:4:2], rden[:, 1:4:2], lamv[:, 0:1], None, ALU.mult).then_inc(inverted, 1)
                ve.wait_ge(inverted, 2 * a + 2)
                if a:
                    ve.wait_ge(turned, a)
                for b, cols in enumerate((slice(0, S), slice(S, S + P))):
                    ve.tensor_scalar(am[:, cols], sc[:, 0, cols], rden[:, 2 * b:2 * b + 1], None, ALU.mult).then_inc(map1, 1)
                ve.wait_ge(map1, 2 * a + 2)
                for b, cols in enumerate((slice(0, S), slice(S, S + P))):
                    ve.scalar_tensor_tensor(am[:, cols], sc[:, 1, cols], rden[:, 2 * b + 1:2 * b + 2], am[:, cols],
                                            ALU.mult, ALU.add).then_inc(map2, 1)

            def keep_ssq(n):
                ve.wait_ge(ssq_mm, n + 1)
                if n == 4:
                    ve.wait_ge(mix_f32, 8)
                ve.tensor_copy(ssq[:, n % 4, :], ps[:, 6, 0:S]).then_inc(ssq_kept, 1)

            def invert_head(n):
                ve.wait_ge(head_rms, 1 if n < 4 else 2 if n < 6 else 3)
                ve.reciprocal(ssq[:, n % 4, :], ssq[:, n % 4, :]).then_inc(head_rstd, 1)
                ve.wait_ge(head_rstd, n + 1)

            def mix_attn(n):
                if n:
                    ve.wait_ge(mix_lo, n)
                else:
                    ve.wait_ge(setup, 4)
                for t in range(2):
                    ve.scalar_tensor_tensor(mt[:, t, :], heads[:, 2 * n + t, :], sub[:, t:t + 1], ssq[:, n, :],
                                            ALU.mult, ALU.mult).then_inc(mix_f32, 1)

            def norm_ret(n):
                invert_head(n)
                hs = heads[:, 2 * (n - 4):2 * (n - 4) + 2, :]
                r = ssq[:, n - 4, :].unsqueeze(1).to_broadcast([P, 2, S])
                ve.tensor_tensor(hs, hs, r, ALU.mult).then_inc(ret_normed, 1)

            def mix_ret(n):
                i = n - 4
                ve.wait_ge(ret_normed, i + 1)
                ve.wait_ge(mix_lo, n)
                ve.wait_ge(gated_r, i // 2 + 1)
                ve.tensor_tensor(mt[:, :, :], heads[:, 2 * i:2 * i + 2, :], gate[:, 2 * i:2 * i + 2, :],
                                 ALU.mult).then_inc(mix_f32, 2)

            def mixed_lo(n):
                ve.wait_ge(mix_hi, n + 1)
                ve.wait_ge(mix_f32, 2 * (n + 1))
                ve.tensor_tensor(mixed[:, 2 * n:2 * n + 2, S:2 * S], mt[:, :, :], mixed[:, 2 * n:2 * n + 2, 0:S].bitcast(F32),
                                 ALU.subtract).then_inc(mix_lo, 1)

            def decay_scores(r):
                ve.wait_ge(rscore_mm, r + 1)
                ve.wait_ge(head_mm, 4 + r)
                if r == 0:
                    ve.wait_ge(map2, 8)
                    ve.wait_ge(table_in, 16 * N_TABLE)
                ve.tensor_tensor(sc[:, 0, 0:S], ps[:, 4, 0:S], dec[:, r, :], ALU.mult).then_inc(decayed, 1)
                ve.tensor_tensor(sc[:, 0, S:S + P], ps[:, 4, S:S + P], dec[:, r, 0:P], ALU.mult).then_inc(decayed, 1)

            def add_mixed(g):
                ve.wait_ge(w_used, KT * (U_OUT + 4 * (g + 1)))
                xs = x[:, 4 * g:4 * g + 4, :]
                acc = narrow(G_OUT + g).rearrange("p b (t s) -> p (b t) s", t=2)
                ve.tensor_tensor(xs, acc, xs, ALU.add).then_inc(evacuated, 1)

            ve.memset(ones[:, :], 1.0).then_inc(setup, 1)
            ve.memset(eps[:, :], EPS).then_inc(setup, 1)
            ve.memset(relb[NB:NB + 1, :], 1.0).then_inc(setup, 1)
            for kt in range(KT):
                h_lo_group(0, 0, 0, [kt])
                w_lo(0, 0, 0, [kt])
            for n in range(1, 4):
                h_lo_group(0, n, 0)
                w_lo(n, 0, n)
            for n in range(4, U_OUT):
                w_lo(n, 0, n % 4)
                if n == 5:
                    ve.wait_ge(c_in, 16 * N_CONST)
                    ve.tensor_tensor(lamp[:, 0:2], lamv[:, 0:2], lamv[:, 2:4], ALU.mult).then_inc(lam_prod, 1)
                    ve.tensor_scalar(sub[:, :], sub[:, :], 1.0 - LAM_INIT, None, ALU.mult).then_inc(setup, 1)
                if n == 6:
                    invert(0)
                    take_out(0)
                if n == 9:
                    ve.wait_ge(lam_exp, 1)
                    ve.tensor_tensor(lamv[:, 1:2], lamp[:, 3:4], lamp[:, 2:3], ALU.subtract).then_inc(lam_done, 1)
                    ve.wait_ge(lam_done, 1)
                    ve.tensor_scalar(lamv[:, 0:1], lamv[:, 1:2], -LAM_INIT, None, ALU.add).then_inc(lam_done, 1)
                if n > 4 and n % 4 == 0:
                    take_out(n // 4 - 1)
                for a, at in enumerate(ATTN_START):
                    if n == at + 1:
                        softmax_front(a)
                    if n == at + 2:
                        softmax_back(a)
                    if n == at + 5:
                        keep_ssq(a)
                for r, at in enumerate(RET_START):
                    if n == at + 1:
                        decay_scores(r)
                    if n == at + 3:
                        keep_ssq(4 + r)
                if n in (35, 37, 39, 41):
                    mixed_lo((n - 35) // 2)
                if n in (33, 35, 37, 39):
                    invert_head((n - 33) // 2)
                if n in (34, 36, 38, 40):
                    mix_attn((n - 34) // 2)
                if n in (47, 49):
                    norm_ret(4 + (n - 47) // 2)
                if n == 54:
                    norm_ret(6)
                if n == 55:
                    mix_ret(4)
                    norm_ret(7)
            for n in range(16):
                w_lo(U_OUT + n, 0, n % 4)
                if n == 0:
                    take_out(13)
                    mixed_lo(4)
                    mix_ret(5)
                if n == 1:
                    mixed_lo(5)
                    mix_ret(6)
                if n == 2:
                    mixed_lo(6)
                    mix_ret(7)
                    mixed_lo(7)
                if n >= 4 and n % 4 == 0:
                    add_mixed(n // 4 - 1)
                if n >= 4 and n % 4 == 1:
                    h_lo_group(1, n // 4 - 1, 1)

            def up_sum(q, Gv, Gp):
                b = wide_bank(Gp)
                ve.wait_ge(sum_a, q + 1)
                ve.tensor_tensor(u[:, :, :], u[:, :, :], ps[:, b:b + 4, S:2 * S], ALU.add).then_inc(evacuated, 1)
                ve.wait_ge(evacuated, Gv + 1)
                ve.tensor_tensor(u[:, :, :], u[:, :, :], rstd_4, ALU.mult).then_inc(u_ready, 1)

            def tap1(q, i, l, gt):
                y = yg if gt else yv
                for m in range(4):
                    t = i * 4 + gt * FT + m
                    ve.wait_ge(y0, q * 4 + m + 1)
                    ve.scalar_tensor_tensor(y[:, m, 1:S], u[:, m, 0:S - 1], cw[:, l, bass.ds(t, 1), 1], y[:, m, 1:S],
                                            ALU.mult, ALU.add).then_inc(y1, 1)

            def tap0(q, i, l, gt):
                y = yg if gt else yv
                for m in range(4):
                    t = i * 4 + gt * FT + m
                    ve.wait_ge(y1, q * 4 + m + 1)
                    ve.scalar_tensor_tensor(y[:, m, 2:S], u[:, m, 0:S - 2], cw[:, l, bass.ds(t, 1), 0], y[:, m, 2:S],
                                            ALU.mult, ALU.add).then_inc(y2, 1)

            def gate_values(p):
                ve.wait_ge(silu_done, p + 1)
                ve.tensor_tensor(yg[:, :, :], yv[:, :, :], yg[:, :, :], ALU.mult).then_inc(gated, 1)

            def act_lo_pair(p, i):
                ve.wait_ge(act_hi, p + 1)
                ve.wait_ge(gated, p + 1)
                ve.tensor_tensor(act[:, bass.ds(i * 4, 4), S:2 * S], yg[:, :, :],
                                 act[:, bass.ds(i * 4, 4), 0:S].bitcast(F32), ALU.subtract).then_inc(act_lo, 1)

            def add_down(l, g):
                ve.wait_ge(w_used, KT * (U_DN[l] + DN_UNITS * (g + 1)))
                b, xs = wide_bank(G_DN[l] + g), x[:, 4 * g:4 * g + 4, :]
                ve.tensor_tensor(xs, ps[:, b:b + 4, 0:S], xs, ALU.add).then_inc(x_half, 1)
                ve.wait_ge(x_half, 4 * l + g + 1)
                ve.tensor_tensor(xs, ps[:, b:b + 4, S:2 * S], xs, ALU.add).then_inc(evacuated, 1)

            for l in range(DEPTH):
                if l == 1:
                    def pool_out(g):
                        ve.wait_ge(pooled_mm, g + 1)
                        b = wide_bank(G_POOL + g) + 2
                        for m in range(4):
                            t = 4 * g + m
                            last = ve.scalar_tensor_tensor(x[:, t, :], ps[:, b + m // 2, (m % 2) * S:(m % 2 + 1) * S],
                                                         pscale[:, t:t + 1], x[:, t, :], ALU.mult, ALU.add)
                        last.then_inc(evacuated, 1)

                    w_lo(U_POOL, 0, 0)
                    add_down(0, 3)
                    h_lo_group(2, 3, 2)
                    w_lo(U_POOL + 1, 0, 1)
                    invert(2)
                    w_lo(U_POOL + 2, 0, 2)
                    pool_out(0)
                    w_lo(U_POOL + 3, 0, 3)
                    h_lo_group(3, 0, 3)
                    pool_out(1)

                def v_windows(i, peel):
                    q = i * 2 + (l * 2 * PAIRS - 1)
                    for j in range(UP_UNITS):
                        w_lo(U_UP[l] + j, i * (8 * KT), j)
                        if peel:
                            if j == 0:
                                if l == 0:
                                    add_mixed(3)
                                else:
                                    h_lo_group(3, 1, 3)
                                    pool_out(2)
                            if j == 1:
                                if l == 0:
                                    h_lo_group(1, 3, 1)
                                else:
                                    h_lo_group(3, 2, 3)
                                    pool_out(3)
                            if j == 2 and l == 1:
                                h_lo_group(3, 3, 3)
                            continue
                        if j == 0:
                            up_sum(q, i * 2 + (G_UP[l] - 1), G_UP[l] - 1)
                        if j == 1:
                            tap1(q, i - 1, l, 1)
                        if j == 2:
                            tap0(q, i - 1, l, 1)
                        if j == 3:
                            gate_values(i + (l * PAIRS - 1))

                def g_windows(i, peel):
                    q = i * 2 + (l * 2 * PAIRS)
                    for j in range(UP_UNITS):
                        w_lo(U_UP[l] + 4 + j, i * (8 * KT), j)
                        if j == 0:
                            if peel:
                                invert(2 * l + 1)
                                ve.wait_ge(rstd_ready, 2 * l + 2)
                            up_sum(q, i * 2 + G_UP[l], G_UP[l])
                        if j == 1:
                            tap1(q, i, l, 0)
                        if j == 2:
                            tap0(q, i, l, 0)
                        if j == 3 and not peel:
                            act_lo_pair(i + (l * PAIRS - 1), i - 1)

                v_windows(0, True)
                g_windows(0, True)
                with ve.Fori(1, PAIRS) as i:
                    v_windows(i, False)
                    g_windows(i, False)
                q = (l + 1) * 2 * PAIRS - 1
                for j in range(DN_UNITS):
                    w_lo(U_DN[l] + j, 0, j % 4)
                    if j == 0:
                        up_sum(q, G_DN[l] - 1, G_DN[l] - 1)
                    if j == 1:
                        tap1(q, PAIRS - 1, l, 1)
                    if j == 2:
                        tap0(q, PAIRS - 1, l, 1)
                    if j == 3:
                        gate_values((l + 1) * PAIRS - 1)
                    if j == 6:
                        act_lo_pair((l + 1) * PAIRS - 1, PAIRS - 1)
                for g in range(1, DN_GROUPS):
                    for j in range(DN_UNITS):
                        w_lo(U_DN[l] + DN_UNITS * g + j, 0, j % 4)
                        if j == 0:
                            add_down(l, g - 1)
                        if j == 2 and l == 0:
                            h_lo_group(2, g - 1, 2)
            ve.wait_ge(w_used, KT * (U_DN[1] + DN_UNITS * DN_GROUPS))
            for half in range(2):
                b, xs = wide_bank(G_DN[1] + 3) + 2 * half, x[:, 12 + 2 * half:14 + 2 * half, :]
                ve.tensor_tensor(xs, ps[:, b:b + 2, 0:S], xs, ALU.add).then_inc(x_half, 1)
                ve.wait_ge(x_half, 4 + 3 + half + 1)
                ve.tensor_tensor(xs, ps[:, b:b + 2, S:2 * S], xs, ALU.add).then_inc(last_added, 1)
            invert(4)
            ve.wait_ge(rstd_ready, 5)
            for t in range(4, DT):
                ve.scalar_tensor_tensor(x[:, t, :], x[:, t, :], gains[:, 4, t:t + 1], rstd_b, ALU.mult, ALU.mult).then_inc(out_ready, 1)

        @block.gpsimd
        def _(pool_e):
            g_ = nc.gpsimd
            rot_n = [0]

            def sum_sq(n):
                if n:
                    pool_e.wait_ge(norm_sum, n)
                g_.memset(sqacc[:, :, :], 0.0).then_inc(sq_added, 1)
                for g in range(SQ_GROUPS[n]):
                    pool_e.wait_ge(sq_ready, 4 * n + g + 1)
                    pool_e.wait_ge(sq_added, SQ_BASE[n] + g + 1)
                    g_.tensor_tensor(sqacc[:, :, :], sqacc[:, :, :], sqt[:, :, :], ALU.add).then_inc(sq_added, 1)
                pool_e.wait_ge(sq_added, SQ_BASE[n + 1] - 2)
                g_.tensor_tensor(sqacc[:, 0:2, :], sqacc[:, 0:2, :], sqacc[:, 2:4, :], ALU.add).then_inc(sq_added, 1)
                pool_e.wait_ge(sq_added, SQ_BASE[n + 1] - 1)
                g_.tensor_tensor(sqacc[:, 0, :], sqacc[:, 0, :], sqacc[:, 1, :], ALU.add).then_inc(sq_added, 1)

            def rotate(buf, i):
                t1, t2 = buf[:, 2 * i, :], buf[:, 2 * i + 1, :]

                def mark(ins):
                    ins.then_inc(rotA, 1)
                    rot_n[0] += 1
                if rot_n[0]:
                    pool_e.wait_ge(rotated, rot_n[0])
                g_.tensor_tensor(rot[:, 0, :], t1, cos[:, :], ALU.mult)
                g_.tensor_tensor(rot[:, 1, :], t2, sin[:, :], ALU.mult)
                g_.tensor_tensor(rot[:, 2, :], t1, sin[:, :], ALU.mult)
                mark(g_.tensor_tensor(t2, t2, cos[:, :], ALU.mult))
                pool_e.wait_ge(rotA, rot_n[0])
                g_.tensor_tensor(t1, rot[:, 0, :], rot[:, 1, :], ALU.subtract)
                g_.tensor_tensor(t2, rot[:, 2, :], t2, ALU.add).then_inc(rotated, 1)

            sum_sq(0)
            pool_e.wait_ge(table_in, 16 * N_TABLE)
            for part in range(2):
                pool_e.wait_ge(evacuated, 6 + 3 * part + 1)
                rotate(qb[part], 0)
                rotate(qb[part], 1)
                pool_e.wait_ge(evacuated, 6 + 3 * part + 2)
                rotate(kb[part], 0)
                rotate(kb[part], 1)
            for n in range(1, 5):
                sum_sq(n)
            pool_e.wait_ge(weighted, 1)
            pool_e.wait_ge(rstd_ready, 5)
            g_.tensor_tensor(x[:, 0:4, :], x[:, 0:4, :], rstd_4, ALU.mult).then_inc(out_pool, 1)


def _constants(S):
    import numpy as np
    nb, max_dist, span = 32, 128, 384
    dist = 255 - np.arange(span)
    d = np.maximum(dist, 0)
    large = 16 + (np.log(np.maximum(d, 1).astype(np.float32) / np.float32(16)) / np.float32(math.log(max_dist / 16))
                  * np.float32(nb - 16)).astype(np.int32)
    bucket = np.where(d < 16, d, np.minimum(large, nb - 1))
    onehot = np.zeros((nb + 1, span), np.float32)
    onehot[bucket[dist >= 0], np.nonzero(dist >= 0)[0]] = 1.0
    onehot[nb, dist < 0] = -1e30
    inv_freq = (1.0 / (np.float32(10000.0) ** np.linspace(0.0, 1.0, 128, dtype=np.float32))).astype(np.float32)
    ang = inv_freq[:, None] * np.arange(S, dtype=np.float32)[None, :]
    g = 1.0 - 2.0 ** (-5.0 - np.arange(4.0))
    rel = np.arange(S)[None, None, :] - np.arange(128)[:, None, None]
    decay = np.where(rel >= 0, g[None, :, None] ** np.maximum(rel, 0), 0.0) / 16.0
    lag = np.arange(S)[None, :] - np.arange(S)[:, None]
    pool = np.stack([((lag >= 0) & (lag < w)) / np.minimum(np.arange(1, S + 1), w)[None, :] - (lag == 0)
                     for w in POOL_WINDOWS], axis=1).astype(np.float32)
    return {
        "bucket_onehot": onehot,
        "rot_cos": np.cos(ang.astype(np.float64)).astype(np.float32),
        "rot_sin": np.sin(ang.astype(np.float64)).astype(np.float32),
        "decay": decay.astype(np.float32),
        "pool_matrix": np.concatenate([pool[:128], pool[128:, :, 128:]], axis=2),
        "ident": np.eye(128, dtype=np.float32),
    }


def kernel(**inputs):
    import numpy as np
    import concourse.bacc as _bacc
    from concourse.bass_utils import run_bass_kernel_spmd as _run

    a = {k: np.asarray(v) for k, v in inputs.items()}
    depth = a["w_up"].shape[0]
    S = a["x"].shape[1]

    def by_partition(v):
        return np.moveaxis(v.reshape(*v.shape[:-1], -1, 128), -1, 0)

    consts = _constants(S)
    norms = np.stack([a["mix_norm"][0], a["ffn_norm"][0], a["mix_norm"][1], a["ffn_norm"][1], a["final_norm"]])
    conv = np.concatenate([a["conv_w"], a["conv_b"][:, None, :]], axis=1)
    arrays = {
        "xT": a["x"][0].T,
        "rel_bias": a["rel_bias"],
        "norm_g": by_partition(norms),
        "w_in": a["w_in"],
        "w_out": a["w_out"],
        "lam": np.stack([a["lam_q1"][0], a["lam_q2"][0], a["lam_k1"][0], a["lam_k2"][0]], axis=1),
        "subln": by_partition(a["diff_subln"][0]),
        "pool_w": a["pool_w"],
        "pool_scale": by_partition(a["pool_scale"][0]),
        "w_up": a["w_up"],
        "conv": np.moveaxis(by_partition(conv), 2, -1),
        "w_down": a["w_down"],
        "bucket_onehot": consts["bucket_onehot"],
        "rot_cos": consts["rot_cos"],
        "rot_sin": consts["rot_sin"],
        "decay": consts["decay"],
        "pool_matrix": consts["pool_matrix"],
        "ident": consts["ident"],
        "flip": consts["ident"][::-1],
    }
    nc = _bacc.Bacc("TRN2", target_bir_lowering=False, num_devices=1, dynamic_dma_scratch_size=4096)
    feed, args = {}, []
    for name, v in arrays.items():
        v = np.ascontiguousarray(v)
        feed[f"in_{name}"] = v
        args.append(nc.dram_tensor(f"in_{name}", v.shape, mybir.dt.from_np(v.dtype), kind="ExternalInput").ap())
    out = nc.dram_tensor("out_T", (a["x"].shape[2], S), F32, kind="ExternalOutput").ap()
    trunk_kernel(nc, *args, out)
    r = _run(nc, [feed], core_ids=[0])
    return np.ascontiguousarray(r.results[0]["out_T"].T)[None]
```
